# Optimizing a Trainium2 kernel written in Bass

```python
import math
import jax, jax.numpy as jnp
from jax import lax
import numpy as np

D_MODEL = 1024
BATCH = 1
SEQ = 512
DEPTH = 2

D_MIX = D_MODEL
HEAD_DIM = 64
DIFF_HEADS = D_MIX // 256
DIFF_QK_DIM = HEAD_DIM
DIFF_V_DIM = 2 * HEAD_DIM
DSA_HEADS = D_MIX // 256
DSA_DIM = HEAD_DIM
IDX_HEADS = D_MIX // 128
IDX_DIM = HEAD_DIM
FOX_HEADS = D_MIX // 256
FOX_DIM = HEAD_DIM
DIFF_WIDTH = DIFF_HEADS * DIFF_V_DIM
DSA_WIDTH = DSA_HEADS * DSA_DIM
FOX_WIDTH = FOX_HEADS * FOX_DIM
DSA_TOPK_MAX = 256
Q_BLOCK = 128
ROPE_THETA = 10000.0
LN_EPS = 1e-5
SUBLN_EPS = 1e-5
NEG_INF = -1e30
DEEPNORM_ALPHA = (2 * DEPTH) ** 0.25
DEEPNORM_BETA = (8 * DEPTH) ** -0.25
IDX_WEIGHT_SCALE = (IDX_HEADS * IDX_DIM) ** -0.5

IN_SPLITS = (
    ('diff_q', DIFF_HEADS * 2 * DIFF_QK_DIM),
    ('diff_k', DIFF_HEADS * 2 * DIFF_QK_DIM),
    ('diff_v', DIFF_HEADS * DIFF_V_DIM),
    ('dsa_q', DSA_HEADS * DSA_DIM),
    ('dsa_k', DSA_DIM),
    ('dsa_v', DSA_DIM),
    ('idx_q', IDX_HEADS * IDX_DIM),
    ('idx_k', IDX_DIM),
    ('idx_w', IDX_HEADS),
    ('fox_q', FOX_HEADS * FOX_DIM),
    ('fox_k', FOX_HEADS * FOX_DIM),
    ('fox_v', FOX_HEADS * FOX_DIM),
    ('fox_f', FOX_HEADS),
    ('gate', D_MIX),
)
VALUE_COLS = ('diff_v', 'dsa_v', 'fox_v')
IN_WIDTH = sum(n for _, n in IN_SPLITS)


def split_columns(h):
    out, off = [], 0
    for _, n in IN_SPLITS:
        out.append(h[..., off:off + n])
        off += n
    return out

def rope(x, pos):
    d = x.shape[-1]
    inv = ROPE_THETA ** (-jnp.arange(0, d, 2, dtype=jnp.float32) / d)
    ang = pos.astype(jnp.float32)[:, None] * inv[None, :]
    shp = (x.shape[1],) + (1,) * (x.ndim - 3) + (d // 2,)
    cos = jnp.cos(ang).reshape(shp).astype(x.dtype)
    sin = jnp.sin(ang).reshape(shp).astype(x.dtype)
    x1, x2 = x[..., : d // 2], x[..., d // 2:]
    return jnp.concatenate([x1 * cos - x2 * sin, x2 * cos + x1 * sin], axis=-1)

def to_blocks(a):
    B, S = a.shape[:2]
    return jnp.moveaxis(a.reshape((B, S // Q_BLOCK, Q_BLOCK) + a.shape[2:]), 1, 0)

def from_blocks(a):
    nb, B, qb = a.shape[:3]
    return jnp.moveaxis(a, 0, 1).reshape((B, nb * qb) + a.shape[3:])

def layer_norm(x, g, b):
    xf = x.astype(jnp.float32)
    mu = jnp.mean(xf, axis=-1, keepdims=True)
    var = jnp.mean(jnp.square(xf - mu), axis=-1, keepdims=True)
    y = (xf - mu) * lax.rsqrt(var + LN_EPS) * g.astype(jnp.float32) + b.astype(jnp.float32)
    return y.astype(x.dtype)

def diff_attention(q, k, v, lam, pos):
    scale = DIFF_QK_DIM ** -0.5
    S = q.shape[1]

    def block(args):
        qb, t = args
        s = jnp.einsum('bqhmd,bkhmd->bhmqk', qb, k).astype(jnp.float32) * scale
        causal = t[:, None] >= pos[None, :]
        p = jax.nn.softmax(jnp.where(causal, s, NEG_INF), axis=-1)
        p = p[:, :, 0] - lam * p[:, :, 1]
        return jnp.einsum('bhqk,bkhe->bqhe', p, v)

    out = lax.map(block, (to_blocks(q), pos.reshape(S // Q_BLOCK, Q_BLOCK)))
    return from_blocks(out)

def dsa_attention(q, k, v, qi, ki, wi, pos, topk):
    scale = DSA_DIM ** -0.5
    S = q.shape[1]

    def block(args):
        qb, qib, wib, t = args
        sc = jnp.einsum('bqhd,bsd->bqhs', qib, ki).astype(jnp.float32)
        idx_score = jnp.einsum('bqhs,bqh->bqs', jax.nn.relu(sc), wib.astype(jnp.float32))
        causal = t[:, None] >= pos[None, :]
        idx_score = jnp.where(causal[None], idx_score, -jnp.inf)
        _, idx = lax.top_k(idx_score, topk)
        kg = jax.vmap(lambda kk, ii: kk[ii])(k, idx)
        vg = jax.vmap(lambda vv, ii: vv[ii])(v, idx)
        s = jnp.einsum('bqhd,bqkd->bhqk', qb, kg).astype(jnp.float32) * scale
        valid = idx <= t[None, :, None]
        p = jax.nn.softmax(jnp.where(valid[:, None], s, NEG_INF), axis=-1)
        return jnp.einsum('bhqk,bqkd->bqhd', p, vg)

    out = lax.map(block, (to_blocks(q), to_blocks(qi), to_blocks(wi),
                          pos.reshape(S // Q_BLOCK, Q_BLOCK)))
    return from_blocks(out)

def forgetting_attention(q, k, v, logf, pos):
    scale = FOX_DIM ** -0.5
    S = q.shape[1]
    c = jnp.cumsum(logf, axis=1)
    c_keys = jnp.transpose(c, (0, 2, 1))

    def block(args):
        qb, cb, t = args
        s = jnp.einsum('bqhd,bkhd->bhqk', qb, k).astype(jnp.float32) * scale
        s = s + jnp.transpose(cb, (0, 2, 1))[..., None] - c_keys[:, :, None, :]
        causal = t[:, None] >= pos[None, :]
        p = jax.nn.softmax(jnp.where(causal, s, NEG_INF), axis=-1)
        return jnp.einsum('bhqk,bkhd->bqhd', p, v)

    out = lax.map(block, (to_blocks(q), to_blocks(c), pos.reshape(S // Q_BLOCK, Q_BLOCK)))
    return from_blocks(out)

def hybrid_layer(x, w_in, b_f, lam_q1, lam_k1, lam_q2, lam_k2, g_subln, w_out, ln_g, ln_b, layer_idx):
    B, S, _ = x.shape
    pos = jnp.arange(S, dtype=jnp.int32)
    h = jnp.einsum('bsd,de->bse', x, w_in)
    (dq, dk, dv, sq, sk, sv, iq, ik, iw, fq, fk, fv, ff, gate) = split_columns(h)

    dq = rope(dq.reshape(B, S, DIFF_HEADS * 2, DIFF_QK_DIM), pos).reshape(B, S, DIFF_HEADS, 2, DIFF_QK_DIM)
    dk = rope(dk.reshape(B, S, DIFF_HEADS * 2, DIFF_QK_DIM), pos).reshape(B, S, DIFF_HEADS, 2, DIFF_QK_DIM)
    dv = dv.reshape(B, S, DIFF_HEADS, DIFF_V_DIM)
    lambda_init = 0.8 - 0.6 * math.exp(-0.3 * layer_idx)
    lam = (jnp.exp(jnp.sum(lam_q1.astype(jnp.float32) * lam_k1.astype(jnp.float32)))
           - jnp.exp(jnp.sum(lam_q2.astype(jnp.float32) * lam_k2.astype(jnp.float32))) + lambda_init)
    a = diff_attention(dq, dk, dv, lam, pos)
    a = a * lax.rsqrt(jnp.mean(a * a, axis=-1, keepdims=True) + SUBLN_EPS) * g_subln.astype(jnp.float32) * (1.0 - lambda_init)
    a = a.reshape(B, S, DIFF_WIDTH)

    sq = rope(sq.reshape(B, S, DSA_HEADS, DSA_DIM), pos)
    sk = rope(sk, pos)
    iq = rope(iq.reshape(B, S, IDX_HEADS, IDX_DIM), pos)
    ik = rope(ik, pos)
    topk = min(DSA_TOPK_MAX, S // 4)
    bo = dsa_attention(sq, sk, sv, iq, ik, iw * IDX_WEIGHT_SCALE, pos, topk).reshape(B, S, DSA_WIDTH)

    logf = jax.nn.log_sigmoid(ff.astype(jnp.float32) + b_f.astype(jnp.float32))
    co = forgetting_attention(fq.reshape(B, S, FOX_HEADS, FOX_DIM), fk.reshape(B, S, FOX_HEADS, FOX_DIM),
                              fv.reshape(B, S, FOX_HEADS, FOX_DIM), logf, pos).reshape(B, S, FOX_WIDTH)

    mixed = jnp.concatenate([a, bo, co], axis=-1) * jax.nn.silu(gate.astype(jnp.float32))
    out = jnp.einsum('bse,ed->bsd', mixed.astype(x.dtype), w_out)
    return layer_norm(DEEPNORM_ALPHA * x + out, ln_g, ln_b)

def first_inputs(seed: int = 0) -> dict:
    key = jax.random.key(seed)
    ks = jax.random.split(key, 12)
    x = jax.random.normal(ks[0], (BATCH, SEQ, D_MODEL), jnp.float32)
    col_scale = np.concatenate([
        np.full((n,), DEEPNORM_BETA if name in VALUE_COLS else 1.0, np.float32) for name, n in IN_SPLITS
    ]) * np.float32(D_MODEL ** -0.5)
    w_in = jax.random.normal(ks[1], (DEPTH, D_MODEL, IN_WIDTH), jnp.float32) * jnp.asarray(col_scale)
    b_f = 1.0 + 0.1 * jax.random.normal(ks[2], (DEPTH, FOX_HEADS), jnp.float32)
    lam_q1 = 0.1 * jax.random.normal(ks[3], (DEPTH, DIFF_QK_DIM), jnp.float32)
    lam_k1 = 0.1 * jax.random.normal(ks[4], (DEPTH, DIFF_QK_DIM), jnp.float32)
    lam_q2 = 0.1 * jax.random.normal(ks[5], (DEPTH, DIFF_QK_DIM), jnp.float32)
    lam_k2 = 0.1 * jax.random.normal(ks[6], (DEPTH, DIFF_QK_DIM), jnp.float32)
    g_subln = 1.0 + 0.02 * jax.random.normal(ks[7], (DEPTH, DIFF_V_DIM), jnp.float32)
    w_out = jax.random.normal(ks[8], (DEPTH, D_MIX, D_MODEL), jnp.float32) * (D_MIX ** -0.5) * DEEPNORM_BETA
    ln_g = 1.0 + 0.02 * jax.random.normal(ks[9], (DEPTH, D_MODEL), jnp.float32)
    ln_b = 0.02 * jax.random.normal(ks[10], (DEPTH, D_MODEL), jnp.float32)
    return {'x': x, 'w_in': w_in, 'b_f': b_f, 'lam_q1': lam_q1, 'lam_k1': lam_k1,
            'lam_q2': lam_q2, 'lam_k2': lam_k2, 'g_subln': g_subln, 'w_out': w_out,
            'ln_g': ln_g, 'ln_b': ln_b}

def first_block(x, w_in, b_f, lam_q1, lam_k1, lam_q2, lam_k2, g_subln, w_out, ln_g, ln_b):
    for l in range(DEPTH):
        x = hybrid_layer(x, w_in[l], b_f[l], lam_q1[l], lam_k1[l], lam_q2[l], lam_k2[l],
                         g_subln[l], w_out[l], ln_g[l], ln_b[l], l)
    return x


GRID_W = 64
CTX_LEN = 256
N_MIXERS = 3
N_HEADS = 16
N_KV_HEADS = 4
HEAD_DIM_2 = D_MODEL // N_HEADS
Q_PER_KV = N_HEADS // N_KV_HEADS
QKV_DIM = (N_HEADS + 2 * N_KV_HEADS) * HEAD_DIM_2
ATTN_SCALE = HEAD_DIM_2 ** -0.5
BLOCK_Q = 128
WINDOW = 128
NA_WIN_H = 8
NA_WIN_W = 16
N_GROUPS = 4
EXPERTS_PER_GROUP = 8
N_EXPERTS = N_GROUPS * EXPERTS_PER_GROUP
TOP_K_IN_GROUP = 2
EXPERT_HIDDEN = D_MODEL // 2
MOE_BLOCK = 128
NORM_EPS = 1e-6
NEG_INF_2 = -1e30
N_A_LAYERS = (DEPTH + N_MIXERS - 1) // N_MIXERS
N_B_LAYERS = (DEPTH + N_MIXERS - 2) // N_MIXERS
N_C_LAYERS = DEPTH // N_MIXERS


def _rmsnorm(x, g):
    x32 = x.astype(jnp.float32)
    y = x32 * lax.rsqrt(jnp.mean(x32 * x32, axis=-1, keepdims=True) + NORM_EPS)
    return (y * g.astype(jnp.float32)).astype(x.dtype)

def _modulate(h, shift, scale):
    return h * (1 + scale) + shift

def _axial_rope_tables(n, dtype):
    t = jnp.arange(n)
    row = (t // GRID_W).astype(jnp.float32)
    col = (t % GRID_W).astype(jnp.float32)
    quarter = HEAD_DIM_2 // 4
    inv = ROPE_THETA ** (-jnp.arange(quarter, dtype=jnp.float32) / quarter)
    ar = row[:, None] * inv
    ac = col[:, None] * inv
    ang = jnp.concatenate([ar, ar, ac, ac], axis=-1)
    return jnp.cos(ang).astype(dtype), jnp.sin(ang).astype(dtype)

def _rot_axial(x):
    r1, r2, c1, c2 = jnp.split(x, 4, axis=-1)
    return jnp.concatenate([-r2, r1, -c2, c1], axis=-1)

def _apply_rope(x, cos, sin):
    shp = (1, x.shape[1]) + (1,) * (x.ndim - 3) + (HEAD_DIM_2,)
    return x * cos.reshape(shp) + _rot_axial(x) * sin.reshape(shp)

def _split_qkv(h, w_qkv):
    b, n, _ = h.shape
    qkv = h @ w_qkv
    q, k, v = jnp.split(qkv, [N_HEADS * HEAD_DIM_2, (N_HEADS + N_KV_HEADS) * HEAD_DIM_2], axis=-1)
    return (q.reshape(b, n, N_KV_HEADS, Q_PER_KV, HEAD_DIM_2),
            k.reshape(b, n, N_KV_HEADS, HEAD_DIM_2),
            v.reshape(b, n, N_KV_HEADS, HEAD_DIM_2))

def _sink_column(sink, lead_shape):
    return jnp.broadcast_to(sink.astype(jnp.float32).reshape(1, N_KV_HEADS, Q_PER_KV, 1, 1), lead_shape + (1,))

def _joint_softmax(s_lat, s_ctx, sink):
    parts = [s_lat, s_ctx]
    if sink is not None:
        parts.append(_sink_column(sink, s_lat.shape[:-1]))
    p = jax.nn.softmax(jnp.concatenate(parts, axis=-1), axis=-1)
    k1 = s_lat.shape[-1]
    c = s_ctx.shape[-1]
    return p[..., :k1], p[..., k1:k1 + c]

def _ctx_self_attention(qc, kc, vc, sink):
    b, n = qc.shape[:2]
    s = jnp.einsum('bqhgd,bkhd->bhgqk', qc, kc).astype(jnp.float32)
    if sink is not None:
        s = jnp.concatenate([s, _sink_column(sink, s.shape[:-1])], axis=-1)
    p = jax.nn.softmax(s, axis=-1)[..., :kc.shape[1]]
    o = jnp.einsum('bhgqk,bkhd->bqhgd', p.astype(vc.dtype), vc)
    return o.reshape(b, n, N_HEADS * HEAD_DIM_2)

def _mixer_window(q, k, v, kc, vc, sink, cos, sin):
    b, n = q.shape[:2]
    nb = n // BLOCK_Q
    span = BLOCK_Q + 2 * WINDOW
    q_rot = _apply_rope(q, cos, sin)
    pad = ((0, 0), (WINDOW, WINDOW), (0, 0), (0, 0))
    k_pad = jnp.pad(_apply_rope(k, cos, sin), pad)
    v_pad = jnp.pad(v, pad)

    def block(i):
        start = i * BLOCK_Q
        qb = lax.dynamic_slice_in_dim(q_rot, start, BLOCK_Q, 1)
        qpb = lax.dynamic_slice_in_dim(q, start, BLOCK_Q, 1)
        kb = lax.dynamic_slice_in_dim(k_pad, start, span, 1)
        vb = lax.dynamic_slice_in_dim(v_pad, start, span, 1)
        qpos = start + jnp.arange(BLOCK_Q)
        kpos = start - WINDOW + jnp.arange(span)
        mask = ((jnp.abs(kpos[None, :] - qpos[:, None]) <= WINDOW)
                & (kpos >= 0)[None, :] & (kpos < n)[None, :])
        s_lat = jnp.einsum('bqhgd,bkhd->bhgqk', qb, kb).astype(jnp.float32)
        s_lat = jnp.where(mask, s_lat, NEG_INF_2)
        s_ctx = jnp.einsum('bqhgd,bkhd->bhgqk', qpb, kc).astype(jnp.float32)
        p_lat, p_ctx = _joint_softmax(s_lat, s_ctx, sink)
        return (jnp.einsum('bhgqk,bkhd->bqhgd', p_lat.astype(v.dtype), vb)
                + jnp.einsum('bhgqk,bkhd->bqhgd', p_ctx.astype(vc.dtype), vc))

    o = lax.map(block, jnp.arange(nb))
    return jnp.moveaxis(o, 0, 1).reshape(b, n, N_HEADS * HEAD_DIM_2)

def _mixer_global(q, k, v, kc, vc, cos, sin):
    b, n = q.shape[:2]
    nb = n // BLOCK_Q
    q_rot = _apply_rope(q, cos, sin)
    k_rot = _apply_rope(k, cos, sin)

    def block(i):
        start = i * BLOCK_Q
        qb = lax.dynamic_slice_in_dim(q_rot, start, BLOCK_Q, 1)
        qpb = lax.dynamic_slice_in_dim(q, start, BLOCK_Q, 1)
        s_lat = jnp.einsum('bqhgd,bkhd->bhgqk', qb, k_rot).astype(jnp.float32)
        s_ctx = jnp.einsum('bqhgd,bkhd->bhgqk', qpb, kc).astype(jnp.float32)
        p_lat, p_ctx = _joint_softmax(s_lat, s_ctx, None)
        return (jnp.einsum('bhgqk,bkhd->bqhgd', p_lat.astype(v.dtype), v)
                + jnp.einsum('bhgqk,bkhd->bqhgd', p_ctx.astype(vc.dtype), vc))

    o = lax.map(block, jnp.arange(nb))
    return jnp.moveaxis(o, 0, 1).reshape(b, n, N_HEADS * HEAD_DIM_2)

def _na_tables(n):
    rows = n // GRID_W
    wh = min(NA_WIN_H, rows)
    ww = min(NA_WIN_W, GRID_W)
    t = np.arange(n)
    r = t // GRID_W
    cl = t % GRID_W
    rs = np.clip(r - wh // 2, 0, rows - wh)
    cs = np.clip(cl - ww // 2, 0, GRID_W - ww)
    kr = rs[:, None, None] + np.arange(wh)[None, :, None]
    kcol = cs[:, None, None] + np.arange(ww)[None, None, :]
    idx = (kr * GRID_W + kcol).reshape(n, wh * ww)
    rel = ((kr - r[:, None, None] + NA_WIN_H - 1) * (2 * NA_WIN_W - 1)
           + (kcol - cl[:, None, None] + NA_WIN_W - 1)).reshape(n, wh * ww)
    return idx.astype(np.int32), rel.astype(np.int32)

def _mixer_neighbourhood(q, k, v, kc, vc, rpb):
    b, n = q.shape[:2]
    nb = n // BLOCK_Q
    idx, rel = _na_tables(n)
    n_keys = idx.shape[1]
    idx_blocks = jnp.asarray(idx).reshape(nb, BLOCK_Q, n_keys)
    rel_blocks = jnp.asarray(rel).reshape(nb, BLOCK_Q, n_keys)
    rpb_flat = rpb.reshape(N_HEADS, -1)

    def block(args):
        i, idx_b, rel_b = args
        qb = lax.dynamic_slice_in_dim(q, i * BLOCK_Q, BLOCK_Q, 1)
        kg = k[:, idx_b]
        vg = v[:, idx_b]
        bias = rpb_flat[:, rel_b].reshape(N_KV_HEADS, Q_PER_KV, BLOCK_Q, n_keys).astype(jnp.float32)
        s_lat = jnp.einsum('bqhgd,bqkhd->bhgqk', qb, kg).astype(jnp.float32) + bias
        s_ctx = jnp.einsum('bqhgd,bkhd->bhgqk', qb, kc).astype(jnp.float32)
        p_lat, p_ctx = _joint_softmax(s_lat, s_ctx, None)
        return (jnp.einsum('bhgqk,bqkhd->bqhgd', p_lat.astype(v.dtype), vg)
                + jnp.einsum('bhgqk,bkhd->bqhgd', p_ctx.astype(vc.dtype), vc))

    o = lax.map(block, (jnp.arange(nb), idx_blocks, rel_blocks))
    return jnp.moveaxis(o, 0, 1).reshape(b, n, N_HEADS * HEAD_DIM_2)

def _hier_moe(h, w_group, b_group, w_router, b_router, w_gate, w_up, w_down):
    t, d = h.shape
    p_grp = jax.nn.softmax((h @ w_group + b_group).astype(jnp.float32), axis=-1)
    grp = jnp.argmax(p_grp, axis=-1)
    p_top = jnp.take_along_axis(p_grp, grp[:, None], axis=-1)
    lg = (h @ w_router + b_router).astype(jnp.float32).reshape(t, N_GROUPS, EXPERTS_PER_GROUP)
    lg = jnp.take_along_axis(lg, grp[:, None, None], axis=1)[:, 0]
    p_in, e_in = lax.top_k(jax.nn.softmax(lg, axis=-1), TOP_K_IN_GROUP)
    wts = (p_top * p_in / jnp.sum(p_in, axis=-1, keepdims=True)).reshape(-1)
    eid = (grp[:, None] * EXPERTS_PER_GROUP + e_in).reshape(-1).astype(jnp.int32)
    tok = jnp.repeat(jnp.arange(t, dtype=jnp.int32), TOP_K_IN_GROUP)
    n_asg = t * TOP_K_IN_GROUP
    cap = -(-n_asg // MOE_BLOCK) * MOE_BLOCK + N_EXPERTS * MOE_BLOCK
    n_blocks = cap // MOE_BLOCK
    order = jnp.argsort(eid)
    eid_s = eid[order]
    tok_s = tok[order]
    wts_s = wts[order]
    counts = jnp.bincount(eid, length=N_EXPERTS).astype(jnp.int32)
    padded = (counts + MOE_BLOCK - 1) // MOE_BLOCK * MOE_BLOCK
    pad_end = jnp.cumsum(padded)
    pad_start = pad_end - padded
    start = jnp.cumsum(counts) - counts
    dest = pad_start[eid_s] + jnp.arange(n_asg, dtype=jnp.int32) - start[eid_s]
    tok_buf = jnp.full((cap,), t, jnp.int32).at[dest].set(tok_s)
    w_buf = jnp.zeros((cap,), jnp.float32).at[dest].set(wts_s)
    blk_e = jnp.minimum(jnp.searchsorted(pad_end, jnp.arange(n_blocks, dtype=jnp.int32) * MOE_BLOCK, side='right'),
                        N_EXPERTS - 1)
    h_pad = jnp.concatenate([h, jnp.zeros((1, d), h.dtype)], axis=0)
    xb = h_pad[tok_buf].reshape(n_blocks, MOE_BLOCK, d)

    def expert_block(args):
        xe, e = args
        return (jax.nn.silu(xe @ w_gate[e]) * (xe @ w_up[e])) @ w_down[e]

    y = lax.map(expert_block, (xb, blk_e)).reshape(cap, d)
    out = jax.ops.segment_sum(y.astype(jnp.float32) * w_buf[:, None], tok_buf, num_segments=t + 1)
    return out[:t]

def second_inputs(seed: int = 0) -> dict:
    key = jax.random.key(seed)
    ks = jax.random.split(key, 24)

    def nrm(k, shape, s):
        return jax.random.normal(k, shape, jnp.float32) * s

    d, f, hd = D_MODEL, EXPERT_HIDDEN, N_HEADS * HEAD_DIM_2
    return {
        'x': nrm(ks[0], (BATCH, SEQ, d), 1.0),
        'c': nrm(ks[1], (BATCH, d), 1.0),
        'ctx': nrm(ks[2], (BATCH, CTX_LEN, d), 1.0),
        'c_ctx': nrm(ks[3], (d,), 1.0),
        'w_ada': nrm(ks[4], (DEPTH, d, 6 * d), 0.5 * d ** -0.5),
        'b_ada': nrm(ks[5], (DEPTH, 6 * d), 0.02),
        'g_attn': 1.0 + nrm(ks[6], (DEPTH, d), 0.05),
        'w_qkv': nrm(ks[7], (DEPTH, d, QKV_DIM), d ** -0.5),
        'w_o': nrm(ks[8], (DEPTH, hd, d), hd ** -0.5),
        'sink_a': nrm(ks[9], (N_A_LAYERS, N_HEADS), 1.0),
        'gq_b': 1.0 + nrm(ks[10], (N_B_LAYERS, HEAD_DIM_2), 0.05),
        'gk_b': 1.0 + nrm(ks[11], (N_B_LAYERS, HEAD_DIM_2), 0.05),
        'rpb_c': nrm(ks[12], (N_C_LAYERS, N_HEADS, 2 * NA_WIN_H - 1, 2 * NA_WIN_W - 1), 0.5),
        'g_ffn': 1.0 + nrm(ks[13], (DEPTH, d), 0.05),
        'w_group': nrm(ks[14], (DEPTH, d, N_GROUPS), d ** -0.5),
        'b_group': nrm(ks[15], (DEPTH, N_GROUPS), 0.01),
        'w_router': nrm(ks[16], (DEPTH, d, N_EXPERTS), d ** -0.5),
        'b_router': nrm(ks[17], (DEPTH, N_EXPERTS), 0.01),
        'w_gate': nrm(ks[18], (DEPTH, N_EXPERTS, d, f), d ** -0.5),
        'w_up': nrm(ks[19], (DEPTH, N_EXPERTS, d, f), d ** -0.5),
        'w_down': nrm(ks[20], (DEPTH, N_EXPERTS, f, d), f ** -0.5),
        'g_final': 1.0 + nrm(ks[21], (d,), 0.05),
    }

def second_block(x, c, ctx, c_ctx, w_ada, b_ada, g_attn, w_qkv, w_o, sink_a, gq_b, gk_b, rpb_c, g_ffn,
              w_group, b_group, w_router, b_router, w_gate, w_up, w_down, g_final):
    b, n, d = x.shape
    cos, sin = _axial_rope_tables(n, x.dtype)
    silu_c = jax.nn.silu(c)
    silu_cc = jax.nn.silu(c_ctx)
    xc = ctx
    for i in range(DEPTH):
        m = i % N_MIXERS
        j = i // N_MIXERS
        last = i == DEPTH - 1
        mod = (silu_c @ w_ada[i] + b_ada[i])[:, None, :]
        modc = (silu_cc @ w_ada[i] + b_ada[i])[None, None, :]
        sh_a, sc_a, gt_a, sh_f, sc_f, gt_f = jnp.split(mod, 6, axis=-1)
        shc_a, scc_a, gtc_a, shc_f, scc_f, gtc_f = jnp.split(modc, 6, axis=-1)

        h = _modulate(_rmsnorm(x, g_attn[i]), sh_a, sc_a)
        hc = _modulate(_rmsnorm(xc, g_attn[i]), shc_a, scc_a)
        q, k, v = _split_qkv(h, w_qkv[i])
        qc, kc, vc = _split_qkv(hc, w_qkv[i])
        sink = None
        if m == 0:
            sink = sink_a[j]
        elif m == 1:
            q, k = _rmsnorm(q, gq_b[j]), _rmsnorm(k, gk_b[j])
            qc, kc = _rmsnorm(qc, gq_b[j]), _rmsnorm(kc, gk_b[j])
        q = q * ATTN_SCALE
        qc = qc * ATTN_SCALE
        if m == 0:
            o = _mixer_window(q, k, v, kc, vc, sink, cos, sin)
        elif m == 1:
            o = _mixer_global(q, k, v, kc, vc, cos, sin)
        else:
            o = _mixer_neighbourhood(q, k, v, kc, vc, rpb_c[j])
        x = x + gt_a * (o @ w_o[i])
        if not last:
            oc = _ctx_self_attention(qc, kc, vc, sink)
            xc = xc + gtc_a * (oc @ w_o[i])

        hf = _modulate(_rmsnorm(x, g_ffn[i]), sh_f, sc_f).reshape(b * n, d)
        if last:
            tokens = hf
        else:
            hfc = _modulate(_rmsnorm(xc, g_ffn[i]), shc_f, scc_f).reshape(-1, d)
            tokens = jnp.concatenate([hf, hfc], axis=0)
        y = _hier_moe(tokens, w_group[i], b_group[i], w_router[i], b_router[i],
                      w_gate[i], w_up[i], w_down[i]).astype(x.dtype)
        x = x + gt_f * y[:b * n].reshape(b, n, d)
        if not last:
            xc = xc + gtc_f * y[b * n:].reshape(xc.shape)
    return _rmsnorm(x, g_final)


def setup_inputs(seed=0):
    out = dict(first_inputs(seed))
    for name, value in second_inputs(seed + 1).items():
        if name != "x":
            out[name + "_2"] = value
    return out


def reference(
    x, w_in, b_f, lam_q1, lam_k1, lam_q2, lam_k2, g_subln, w_out, ln_g, ln_b, c_2, ctx_2,
    c_ctx_2, w_ada_2, b_ada_2, g_attn_2, w_qkv_2, w_o_2, sink_a_2, gq_b_2, gk_b_2, rpb_c_2,
    g_ffn_2, w_group_2, b_group_2, w_router_2, b_router_2, w_gate_2, w_up_2, w_down_2,
    g_final_2,
):
    x = first_block(
        x, w_in, b_f, lam_q1, lam_k1, lam_q2, lam_k2, g_subln, w_out, ln_g, ln_b,
    )
    return second_block(
        x, c_2, ctx_2, c_ctx_2, w_ada_2, b_ada_2, g_attn_2, w_qkv_2, w_o_2, sink_a_2, gq_b_2,
        gk_b_2, rpb_c_2, g_ffn_2, w_group_2, b_group_2, w_router_2, b_router_2, w_gate_2,
        w_up_2, w_down_2, g_final_2,
    )


_drawn_inputs = setup_inputs


def setup_inputs(seed=0):
    import zlib

    import numpy as np

    out = dict(_drawn_inputs(seed))
    spreads = {}
    factors = {'b_f': 36.799,
     'lam_q1': 3.129,
     'lam_k1': 3.135,
     'lam_q2': 3.63,
     'g_subln': 8.0,
     'g_attn_2': 6.941,
     'sink_a_2': 8.0,
     'gq_b_2': 8.0,
     'gk_b_2': 8.0,
     'b_group_2': 4.978,
     'b_router_2': 7.699}
    for name, (base, spread) in spreads.items():
        noise = np.random.default_rng([zlib.crc32(name.encode()), seed]).standard_normal(out[name].shape)
        drawn = base * np.exp(spread * noise) if base else spread * noise
        out[name] = __import__('jax').numpy.asarray(drawn.astype(out[name].dtype))
    for name, factor in factors.items():
        out[name] = (out[name] * factor).astype(out[name].dtype)
    return out
```

```python
import math
from contextlib import ExitStack

import numpy as np

import concourse.bass as bass
from concourse import mybir

F32 = mybir.dt.float32
BF16 = mybir.dt.bfloat16
I32 = mybir.dt.int32
ALU = mybir.AluOpType
ACT = mybir.ActivationFunctionType
AX = mybir.AxisListType

P = 128
D = 1024
SEQ = 512
CTX = 256
DEPTH = 2
DC = D // P
XT_TILES = SEQ // P
CTX_TILES = CTX // P
HD = 64
SCALE = HD ** -0.5
ALPHA = (2 * DEPTH) ** 0.25
TOPK = min(256, SEQ // 4)
IDX_HEADS = D // 128
IDX_SCALE = (IDX_HEADS * HD) ** -0.5
Q_HEADS, KV_HEADS = 16, 4
GROUPS, PER_GROUP = 4, 8
EXPERTS = GROUPS * PER_GROUP
HIDDEN = D // 2
ROUTER = GROUPS + EXPERTS
TOKENS = SEQ + CTX
MAX_OVER = (2 * TOKENS) // (P + 1)
BLOCKS = EXPERTS + MAX_OVER
BIG = 1e30
HALF_ROWS = P // 2
REPLACED = -3e38
EPS1, EPS2 = 1e-5, 1e-6
THETA = 10000.0

DQ, DK, DV, SQ, SK, SV, IQ, IK, IW, FQ, FK, FV, FF, GATE = np.cumsum(
    [0, 512, 512, 512, 256, 64, 64, 512, 64, 8, 256, 256, 256, 4]).tolist()
CHUNKS = {
    "idx_q": [(IQ, 512)],
    "idx_k": [(IK, 72), (FF, 4), (FV, 256)],
    "dsa": [(SQ, 384)],
    "fox": [(FQ, 512)],
    "diff_q": [(DQ, 512)],
    "diff_k": [(DK, 512)],
    "diff_v": [(DV, 512)],
    "gate0": [(GATE, 512)],
    "gate1": [(GATE + 512, 512)],
}
IN_WIDTH = GATE + D

CONST = {}


def constants():
    cols, at = [], 0

    def put(name, a):
        nonlocal at
        a = np.asarray(a, np.float32).reshape(P, -1)
        CONST[name] = (at, at + a.shape[1])
        at += a.shape[1]
        cols.append(a)

    p = np.arange(P)
    put("ident", np.eye(P))
    put("above", np.where(p[None, :] > p[:, None], BIG, 0.0))
    put("tri", p[:, None] <= p[None, :])
    put("ones", np.ones((P, P)))
    put("below", np.where(p[None, :] < p[:, None], BIG, 0.0))
    put("before", p[:, None] < p[None, :])
    put("tok", p[:, None] + P * np.arange(TOKENS // P)[None, :])
    put("up32", np.tile(np.arange(EXPERTS), (P, 1)))
    put("down32", np.tile(EXPERTS - np.arange(EXPERTS), (P, 1)))
    put("down4", np.tile(GROUPS - np.arange(GROUPS), (P, 1)))
    put("over", np.tile(np.arange(MAX_OVER), (P, 1)))
    pos = np.arange(SEQ).astype(np.float32)
    inv = (np.float32(THETA) ** (-np.arange(0, HD, 2, dtype=np.float32) / np.float32(HD))).astype(np.float32)
    ang = pos[:, None] * inv[None, :]
    ang = np.concatenate([ang, ang], 1)
    sign = np.concatenate([-np.ones(32), np.ones(32)])
    quarter = HD // 4
    inv4 = (np.float32(THETA) ** (-np.arange(quarter, dtype=np.float32) / np.float32(quarter))).astype(np.float32)
    ar = (np.arange(SEQ) // 64).astype(np.float32)[:, None] * inv4
    ac = (np.arange(SEQ) % 64).astype(np.float32)[:, None] * inv4
    ax = np.concatenate([ar, ar, ac, ac], 1)
    sign4 = np.tile(np.concatenate([-np.ones(16), np.ones(16)]), 2)

    def by_tile(a):
        return a.reshape(XT_TILES, P, HD).transpose(1, 0, 2)

    put("rope1", np.stack([by_tile(np.cos(ang)), by_tile(np.sin(ang) * sign)], 1))
    put("rope2", np.stack([by_tile(np.cos(ax)), by_tile(np.sin(ax) * sign4)], 1))
    return np.concatenate(cols, 1)


CONSTANTS = constants()


class Signal:

    def __init__(self, ins, counting):
        self.ins, self.counting = ins, counting

    def then_inc(self, sem, n):
        self.counting.add(sem, n)
        return self.ins.then_inc(sem, n)


class Counting:

    def __init__(self):
        self.count, self.latest = {}, None

    def add(self, sem, n):
        self.count[sem.name] = self.count.get(sem.name, 0) + n
        self.latest = (sem, self.count[sem.name])

    def of(self, make):
        return lambda *a, **k: Signal(make(*a, **k), self)

    def increment(self, engine, sem, n):
        engine.sem_inc(sem, n)
        self.add(sem, n)


class Step:

    def __init__(self, kind, l=None, t=None, h=None, j=None, c=None, e=None, name=None, what=None, ctx=False, last=None,
                 pj=None, tr=None, sc=None, stg=(), fin=None, bc=None, w=None, u=None, f=None, s=None, index=None,
                 ada=None, count=None, rounds=None, block=None, blocks=None, rows=None, lat=None, topk=None,
                 tr_before=None, src_tr=None, after=None, tiles=None, turns=None, slot=None, loads=None, prev=None,
                 cols=None, half=None, base=None, order=None, xe0=None):
        self.kind, self.l, self.t, self.h, self.j, self.c, self.e = kind, l, t, h, j, c, e
        self.name, self.what, self.ctx, self.last = name, what, ctx, last
        self.pj, self.tr, self.sc, self.stg, self.fin, self.bc = pj, tr, sc, stg, fin, bc
        self.w, self.u, self.f, self.s, self.index, self.ada = w, u, f, s, index, ada
        self.count, self.rounds, self.block, self.blocks, self.rows = count, rounds, block, blocks, rows
        self.lat, self.topk, self.tr_before, self.src_tr, self.after = lat, topk, tr_before, src_tr, after
        self.tiles, self.turns = tiles, turns
        self.slot, self.loads, self.prev, self.cols, self.half = slot, loads, prev, cols, half
        self.base, self.order, self.xe0 = base, order, xe0


def make_plan(until=99):
    steps = []
    n = dict(pj=0, tr=0, sc=0, stg=0, unit=0, fin=0, bc=0, topk=0, idx=0, ada=0, mixed=0)
    units = []
    slot_loads = [0] * 6

    def take(what, k=1):
        n[what] += k
        return list(range(n[what] - k, n[what]))

    def weight(kind, **kw):
        slot = weight.at % 3
        weight.at += 1
        prev = weight.last[slot]
        slot_loads[slot] += len(kw.get("cols", (0,)))
        u = Step(kind=kind, index=len(units), slot=slot, loads=slot_loads[slot], prev=prev, **kw)
        weight.last[slot] = u.index
        units.append(u)
        return u

    weight.at, weight.last = 0, [None] * 6

    def add(kind, **kw):
        s = Step(kind=kind, tr_before=n["tr"] - len(kw.get("tr", ())), **kw)
        steps.append(s)
        users = kw.get("w")
        if users is not None and kw.get("last", True):
            for u, use in zip(users if isinstance(users, list) else [users], kw["pj"] if isinstance(kw["pj"], list) else [kw["pj"]]):
                u.done = use + 1
        return s

    def attend(unit_list, extra=None, after=None):
        m = len(unit_list)
        for i in range(m + 2):
            if i < m:
                u = unit_list[i]
                u.sc = take("sc")[0]
                u.index = attend.count
                attend.count += 1
                n["mixed"] += u.kind == "diff"
                u.mixed = n["mixed"]
                u.first = i == 0
                s = add("scores", u=u)
                u.needs = s.tr_before
            if 1 <= i <= m:
                u = unit_list[i - 1]
                u.tr = take("tr", -(-u.blocks // 4))
                add("turn", u=u)
            if i >= 2:
                u = unit_list[i - 2]
                u.pj = take("pj")[0]
                add("weigh", u=u)
                if after and (i - 2) in after:
                    after[i - 2]()
            if extra and i in extra:
                extra[i]()

    attend.count = 0

    for t in range(XT_TILES):
        add("open", t=t, fin=take("fin")[0], tr=take("tr", 2))

    for l in range(DEPTH):
        add("layer1", l=l)
        names = list(CHUNKS)
        topk_left = {t: TOPK // 8 for t in (1, 2, 3)}
        pending = []

        def project(name, t, w, l=l):
            s = add("project", l=l, name=name, t=t, w=w, last=(t == XT_TILES - 1), pj=take("pj")[0], turns=[])
            return s

        def turn_staged(s):
            blocks = {"idx_q": [(8, 4, P)], "idx_k": [(12, 1, P)], "fox": [(16, 4, 66), (20, 4, 66)],
                      "dsa": [(13, 3, P)], "diff_q": [(0, 4, P)], "diff_k": [(4, 4, P)]}.get(s.name, [])
            if s.name == "fox":
                s.stg = take("stg", 2)
            elif blocks:
                s.stg = take("stg", 1)
            pending.append((s, blocks))

        def flush(keep):
            while len(pending) > keep:
                s, blocks = pending.pop(0)
                for k, b in enumerate(blocks):
                    add("stage_turn", s=s, stg=s.stg[k], block=b[0], count=b[1], rows=b[2], tr=take("tr"), l=s.l)

        for ci, name in enumerate(names):
            w = weight("w_in", l=l, cols=CHUNKS[name])
            for t in range(XT_TILES):
                s = project(name, t, w)
                turn_staged(s)
                flush(1)
                if name == "dsa" and t == 0:
                    add("forget", l=l, pj=take("pj")[0])
                if ci >= 2:
                    if ci - 1 in (1, 2, 3):
                        for h in (2 * t, 2 * t + 1):
                            add("index", l=l, t=ci - 1, h=h, sc=take("sc")[0], index=take("idx")[0])
                    for tt in (1, 2, 3):
                        if topk_left[tt] and tt < ci - 1:
                            k = min(4 if ci < 5 else 2, topk_left[tt])
                            topk_left[tt] -= k
                            add("topk", l=l, t=tt, rounds=k, last=topk_left[tt] == 0,
                                count=n["topk"] + (topk_left[tt] == 0))
                            n["topk"] += topk_left[tt] == 0
                            break
            if name == "idx_k":
                add("log_f", l=l)
        flush(0)
        while any(topk_left.values()):
            tt = next(t for t in topk_left if topk_left[t])
            topk_left[tt] = 0
            raise AssertionError("top-k rounds left over")

        unit_list = []
        for t in range(XT_TILES):
            for h in range(4):
                unit_list.append(Step(kind="diff", l=l, t=t, h=h, blocks=t + 1))
            for h in range(4):
                unit_list.append(Step(kind="fox", l=l, t=t, h=h, blocks=t + 1))
            for h in range(4):
                unit_list.append(Step(kind="dsa", l=l, t=t, h=h, blocks=t + 1, topk=3 * l + t))

        def ada(j, l=l):
            def go():
                add("ada", l=l, j=j, w=weight("w_ada", l=l, j=j), pj=take("pj")[0], ada=take("ada")[0])
            return go

        attend(unit_list, extra={4 * j + 3: ada(j) for j in range(12)})
        add("subln", l=l)
        wo = [weight("w_out", l=l, half=h) for h in range(2)]
        bc = take("bc")[0]
        add("load_bc", bc=bc, what="ln", l=l)

        turned = {}

        def mixturn(t, l=l):
            turned[t] = add("mix_turn", t=t, l=l, tr=take("tr", 2)).tr[-1]

        mixturn(0)
        fins = []
        for t in range(XT_TILES):
            if t + 1 < XT_TILES:
                mixturn(t + 1)
            s = add("wout", l=l, t=t, w=wo, last=(t == XT_TILES - 1), pj=take("pj", 2), fin=take("fin")[0], bc=bc,
                    src_tr=turned[t])
            fins.append(s)
            if l == 0 and t:
                add("fin_turn", f=fins[t - 1], tr=take("tr", 2))
        if l == 0:
            add("fin_turn", f=fins[-1], tr=take("tr", 2))
    if until <= 1:
        return steps, units, n

    for l in range(DEPTH):
        last = l == DEPTH - 1
        tiles = XT_TILES + CTX_TILES
        kv_only = CTX_TILES if last else 0
        add("layer2", l=l)
        if l == 0:
            prev = None
            for t in range(tiles):
                if t in (0, XT_TILES):
                    bc = take("bc")[0]
                    add("load_bc", bc=bc, what="attn", l=l, ctx=t >= XT_TILES)
                s = add("norm0", l=l, t=t, fin=take("fin")[0], bc=bc, ctx=t >= XT_TILES)
                if prev:
                    add("fin_turn", f=prev, tr=take("tr", 2))
                prev = s
            add("fin_turn", f=prev, tr=take("tr", 2))
        prev = []

        def flush2(keep):
            while len(prev) > keep:
                add("qk_turn", s=(s := prev.pop(0)), tr=take("tr", s.turns))

        for c, name in enumerate(("q0", "q1", "kv")):
            w = weight("w_qkv", l=l, c=c)
            ts = range(XT_TILES) if (last and c < 2) else range(tiles)
            for t in ts:
                two = c < 2 and t < XT_TILES
                s = add("qkv", l=l, c=c, t=t, w=w, last=t == ts[-1], pj=take("pj")[0], stg=take("stg", 2 if two else 1),
                        turns=2 if two else 1)
                prev.append(s)
                flush2(1)
        flush2(0)
        unit_list = []
        for t in range(XT_TILES if last else tiles):
            for h in range(Q_HEADS):
                if t >= XT_TILES:
                    unit_list.append(Step(kind="ctx", l=l, t=t, h=h, blocks=2, lat=[]))
                elif l % 3 == 0:
                    lat = [b for b in (t - 1, t, t + 1) if 0 <= b < XT_TILES]
                    unit_list.append(Step(kind="window", l=l, t=t, h=h, blocks=2 + len(lat), lat=lat))
                else:
                    unit_list.append(Step(kind="global", l=l, t=t, h=h, blocks=2 + XT_TILES, lat=list(range(XT_TILES))))

        turned = {}

        def oturn(t):
            def go():
                turned[t] = add("o_turn", t=t, after=unit_list[16 * t + 15].pj, tr=take("tr", 2)).tr[-1]
            return go

        attend(unit_list, after={16 * (k + 1) - 1: oturn(k) for k in range(len(unit_list) // 16)})
        wo = [weight("w_o", l=l, half=h) for h in range(2)]
        moe_tiles = XT_TILES if last else tiles
        prev = None
        for t in range(moe_tiles):
            if t in (0, XT_TILES):
                bc = take("bc")[0]
                add("load_bc", bc=bc, what="ffn", l=l, ctx=t >= XT_TILES)
            s = add("wo", l=l, t=t, w=wo, last=(t == moe_tiles - 1), pj=take("pj", 2), fin=take("fin")[0], bc=bc,
                    src_tr=turned[t])
            if prev:
                add("fin_turn", f=prev, tr=take("tr", 2))
            prev = s
        add("fin_turn", f=prev, tr=take("tr", 2))
        add("route", l=l, tiles=moe_tiles, pj=take("pj", 3))
        base = len(units)
        first_wo = wo[0].index
        order = [("gate", 0), ("up", 0)]
        for e in range(EXPERTS):
            if e + 1 < EXPERTS:
                order += [("gate", e + 1), ("up", e + 1)]
            order.append(("down", e))
        for k, (what, e) in enumerate(order):
            slot = k % 6
            slot_loads[slot] += 1
            prev_use = weight.last[slot] if k < 3 else (wo[1].index if k < 6 else base + k - 6)
            u = Step(kind=what, l=l, e=e, index=base + k, slot=slot, loads=slot_loads[slot], prev=prev_use)
            u.done = n["pj"] + 2 * e + 2 if what == "down" else n["sc"] + e + 1
            units.append(u)
            weight.last[slot] = base + k
        weight.at = 0
        add("moe", l=l, tiles=moe_tiles, xe0=[16 * 17 * l] * 2, tr=take("tr", 4 + 3 * EXPERTS - 2), sc=take("sc", EXPERTS), pj=take("pj", 2 * EXPERTS),
            base=base, order=order)
        prev = None
        for t in range(moe_tiles):
            if t in (0, XT_TILES):
                bc = take("bc")[0]
                add("load_bc", bc=bc, what="final" if last else "next", l=l, ctx=t >= XT_TILES)
            s = add("combine", l=l, t=t, fin=take("fin")[0], bc=bc, last=last, tiles=moe_tiles)
            if not last:
                if prev:
                    add("fin_turn", f=prev, tr=take("tr", 2))
                prev = s
        if not last:
            add("fin_turn", f=prev, tr=take("tr", 2))
    return steps, units, n


def finish_plan(steps):
    count = dict(load=[0, 0], xst=[0, 0], hst=[0, 0], q=0, gat=[0, 0], sd=0)
    fins = [s for s in steps if s.kind in FINISHING]
    turned_by = {}
    for s in steps:
        if s.kind == "stage_turn":
            turned_by[s.stg] = s.tr[0]
        if s.kind == "qk_turn":
            for k, use in enumerate(s.tr):
                turned_by[s.s.stg[k]] = use
    for s in fins:
        k = s.fin % 2
        count["load"][k] += 1
        s.load = count["load"][k]
        s.turned = None
        s.stores_x = s.kind == "wout" or s.kind == "wo" or (s.kind == "combine" and not s.last and s.t < XT_TILES)
        s.stores_h = s.kind == "wo" or (s.kind == "combine" and s.last)
        s.normed = s.kind in ("norm0", "wo", "combine")
        count["xst"][k] += s.stores_x
        count["hst"][k] += s.stores_h
        s.xst, s.hst = list(count["xst"]), list(count["hst"])
        if s.kind != "open":
            count["q"] += 1
        s.q = count["q"]
        count["sd"] += s.kind in ("wout", "wo", "combine")
        s.sd = count["sd"]
        if s.kind == "combine":
            count["gat"][k] += 1
        s.gat = list(count["gat"])
    for s in steps:
        if s.kind == "fin_turn":
            s.f.turned = s.tr[-1]
        if s.kind == "open":
            s.turned = s.tr
        if s.kind == "open":
            s.turned = s.tr[-1]
    gates = norms = qn = 0
    ada_dmas = [0, 0]
    bc_dmas = {}
    total_bc = 0
    loaded = 0
    o_turns = []
    opened = {}
    for s in steps:
        if s.kind == "project":
            if s.name in ("gate0", "gate1"):
                gates += 1
                s.gate = gates
        if s.kind in ("norm0", "wo", "combine"):
            norms += 1
            s.normn = norms
        if s.kind == "qkv" and s.l % 3 == 1:
            qn += 1
            s.qn = qn
        if s.kind == "ada":
            ada_dmas[s.ada % 2] += 8 if s.j // 2 in (1, 4) else 4
            s.ada_dmas = ada_dmas[s.ada % 2]
        if s.kind == "load_bc":
            total_bc += {"ln": 2, "attn": 2, "ffn": 3, "next": 3, "final": 2}[s.what]
            bc_dmas[s.bc] = total_bc
        if s.kind in ("wout", "norm0", "wo", "combine"):
            s.bc_dmas = bc_dmas[s.bc]
        if s.kind in ("layer1", "layer2"):
            loaded += 6 if s.kind == "layer1" else 2
            s.loaded = loaded
        if s.kind == "o_turn":
            o_turns.append(s)
        if s.kind == "scores":
            s.u.o_before = o_turns[-2].tr[-1] if s.u.t % 2 == 0 and len(o_turns) >= 2 else (
                o_turns[-2].tr[-1] if len(o_turns) >= 2 else None)
        if s.kind == "moe":
            s.y0 = 256 * s.l
    return fins, turned_by


FINISHING = ("open", "wout", "norm0", "wo", "combine")


def build(nc, ins, out, until=99, debug=None):
    steps, units, totals = make_plan(until)
    fins, turned_by = finish_plan(steps)
    by_fin = {s.fin: s for s in fins}

    ctx = ExitStack()
    with ctx:
        def sb(name, words, dt=F32):
            return ctx.enter_context(nc.sbuf_tensor(name, [P, words], dt))[:, :]

        def sem(name):
            return ctx.enter_context(nc.semaphore(name))

        XT = sb("XT", DC * TOKENS)
        G = sb("G", 4 * D)
        WR = sb("WR", 3 * DC * 512)
        QK = sb("QK", 24 * 512)
        V = sb("V", 4 * 832)
        XS = sb("XS", 2 * D)
        STG = sb("STG", 2 * 640)
        TMP = sb("TMP", 2 * 512)
        PR = sb("PR", 2 * 1024)
        PT = sb("PT", 2 * 768)
        BC = sb("BC", 3 * D)
        SEL = sb("SEL", 1152, BF16)
        KF = sb("KF", 4 * P)
        KB = sb("KB", 5 * P, BF16)
        ROPE = sb("ROPE", 2 * XT_TILES * HD)
        GSUB = sb("GSUB", P)
        SM = sb("SM", 1160)
        SMI = ctx.enter_context(nc.sbuf_tensor("SMI", [P, 80], I32))

        at = [0]

        def small(n):
            at[0] += n
            assert at[0] <= 1160
            return SM[:, at[0] - n:at[0]]

        LAMV, NLAM, LAMS = small(256), small(1), small(4)
        WIDX, FFZ, CUM = small(32), small(16), small(16)
        FT = [small(16) for _ in range(4)]
        XI = SMI[:, 76:78]
        BFT = small(4)
        NM, LS, RI, CC = small(8), small(8), small(8), small(4)
        M8, SS, RS = small(8), small(16), small(16)
        STATS, AGG, RSTD, STD = small(24), small(4), small(2), small(2)
        EPS = small(2)
        RWT, RB = small(DC * ROUTER), small(ROUTER)
        TABLES = small(CONST["over"][1] - CONST["tok"][0])
        TOK, U32T, D32T, D4T, OVT = (TABLES[:, CONST[k][0] - CONST["tok"][0]:CONST[k][1] - CONST["tok"][0]]
                                     for k in ("tok", "up32", "down32", "down4", "over"))
        total_ids = [0]
        W12 = small(2 * 6)
        SCT, SCR = small(2 * DC), small(2 * DC)
        QN = small(48)
        IDX, DEST, OVI = SMI[:, 0:BLOCKS], SMI[:, 44:56], SMI[:, 60:61 + MAX_OVER]
        identF, aboveF, triF, onesF = (KF[:, k * P:(k + 1) * P] for k in range(4))
        identB, aboveB, belowB, beforeB, onesB = (KB[:, k * P:(k + 1) * P] for k in range(5))

        def slot_tile(slot):
            base = WR if slot < 3 else QK
            k = slot % 3
            return base[:, k * 4096:(k + 1) * 4096]

        XT1 = XT[:, 0:DC * SEQ].rearrange("p (c n) -> p c n", c=DC)
        ARAW = XT[:, DC * SEQ:DC * SEQ + 4 * 512]
        XT2 = XT[:, :].rearrange("p (c n) -> p c n", c=DC)
        blk = QK[:, :].rearrange("p (b n) -> p b n", n=512)
        KX = BC[:, 2 * D:3 * D].rearrange("p (b n) -> p b n", n=512)
        G1 = G[:, :].rearrange("p (t n) -> p t n", n=D)
        O2 = G1[:, 0:2]
        HS = G1[:, 2:4]
        V1d = V[:, 0:2048].rearrange("p (t n) -> p t n", t=4)
        V1s = V[:, 2048:2304].rearrange("p (t n) -> p t n", t=4)
        V1f = V[:, 2304:3328].rearrange("p (t n) -> p t n", t=4)
        V2 = V[:, 0:6 * 256].rearrange("p (t n) -> p t n", t=6)
        Wk = {1: BC[:, 0:256], 2: BC[:, 256:640], 3: BC[:, 640:1152]}
        SELt = {1: SEL[:, 0:256], 2: SEL[:, 256:640], 3: SEL[:, 640:1152]}
        REL = [PT[:, 0:512], PT[:, 768:1280]]
        ropeC = ROPE[:, 0:XT_TILES * HD].rearrange("p (t n) -> p t n", n=HD)
        ropeS = ROPE[:, XT_TILES * HD:].rearrange("p (t n) -> p t n", n=HD)
        JUNK = PT[:, 0:D]
        QROT = QK[:, 0:4096].rearrange("p (b n) -> p b n", n=SEQ)
        QPLAIN = QK[:, 4096:8192].rearrange("p (b n) -> p b n", n=SEQ)
        QCTX = QK[:, 8192:10240].rearrange("p (b n) -> p b n", n=CTX)
        KROT = QK[:, 10240:12288].rearrange("p (g n) -> p g n", n=SEQ)
        KCTX = V[:, 1536:2560].rearrange("p (g n) -> p g n", n=CTX)
        XE = [XT[:, k * D:(k + 1) * D] for k in range(2)]
        XET = [XT[:, (2 + k) * D:(3 + k) * D].rearrange("p (c n) -> p c n", c=DC) for k in range(2)]
        YR = [XT[:, (4 + k) * D:(5 + k) * D] for k in range(2)]
        GSI = [G[:, k * 512:(k + 1) * 512] for k in range(2)]
        UPS = [G[:, (2 + k) * 512:(3 + k) * 512] for k in range(2)]
        HID = [PR[:, k * 1024:k * 1024 + 512] for k in range(2)]
        HTD = [PT[:, k * 768:k * 768 + 512].rearrange("p (c n) -> p c n", c=4) for k in range(2)]
        RT, o = {}, 0
        for name, n in (("g4", 24), ("ge", 24), ("oh4", 24), ("l", 192), ("eq", 192), ("oh1", 192), ("oh2", 192),
                        ("rk", 192), ("eq32", MAX_OVER * EXPERTS), ("cn", 32), ("nb", 32), ("incl", 32), ("ob", 32),
                        ("mb", 32), ("t0", 6), ("t1", 6), ("m1", 6), ("m2", 6), ("e2", 6), ("r", 6), ("o", 6), ("m", 6),
                        ("be", MAX_OVER)):
            RT[name] = PR[:, o:o + n]
            o += n
        YG = [PR[:, :].rearrange("p (k n) -> p k n", k=2), V[:, 0:2048].rearrange("p (k n) -> p k n", k=2)]

        SC = ctx.enter_context(nc.psum_tensor("SC", [P, 2, 1024], F32))
        TR = ctx.enter_context(nc.psum_tensor("TR", [P, 2, 512], F32))
        PJ = ctx.enter_context(nc.psum_tensor("PJ", [P, 2, 512], F32))

        def dram(name, shape):
            return nc.dram_tensor(name, shape, F32, kind="ExternalOutput" if debug and name in debug else "Internal").ap()

        XD = dram("x_rows", (TOKENS, D))
        HDR = dram("h_rows", (TOKENS, D))
        YD = dram("y_rows", (BLOCKS * P, D))
        IDT = dram("slot_tokens", (BLOCKS * P, 1))
        MOD = dram("modulation", (DEPTH, 2, 6 * D))

        w_loaded = [sem(f"w_loaded{k}") for k in range(6)]
        sink_ready = sem("sink_ready")
        pj_full, pj_free = sem("pj_full"), sem("pj_free")
        tr_full, tr_free = sem("tr_full"), sem("tr_free")
        sc_full, sc_free = sem("sc_full"), sem("sc_free")
        dve_done, act_done = sem("dve_done"), sem("act_done")
        stg_ready, nm_ready, mixed_ready = sem("stg_ready"), sem("nm_ready"), sem("mixed_ready")
        rel_used, topk_done = sem("rel_used"), sem("topk_done")
        fox_in, fox_exp, fox_one, fox_ln, logf_ready = (sem(k) for k in ("fox_in", "fox_exp", "fox_one", "fox_ln", "logf_ready"))
        lam_in, lam_exp = sem("lam_in"), sem("lam_exp")
        gate_raw, gate_ready = sem("gate_raw"), sem("gate_ready")
        sub_in, sub_out, sub_done = sem("sub_in"), sem("sub_out"), sem("sub_done")
        consts_loaded, kb_ready, idt_zeroed = sem("consts_loaded"), sem("kb_ready"), sem("idt_zeroed")
        zeros_ready, yd_zeroed = sem("zeros_ready"), sem("yd_zeroed")
        pool_done, gather_started = sem("pool_done"), sem("gather_started")
        layer_loaded, rope2_loaded, router_loaded = sem("layer_loaded"), sem("rope2_loaded"), sem("router_loaded")
        c_loaded, c_silu = sem("c_loaded"), sem("c_silu")
        ada_loaded = [sem(f"ada_loaded{k}") for k in range(2)]
        ada_ready = sem("ada_ready")
        mod_stored = [sem(f"mod_stored{k}") for k in range(2)]
        xs_loaded = [sem(f"xs_loaded{k}") for k in range(2)]
        bc_loaded = sem("bc_loaded")
        std_in, std_ready, fin_done = sem("std_in"), sem("std_ready"), sem("fin_done")
        x_stored = [sem(f"x_stored{k}") for k in range(2)]
        h_stored = [sem(f"h_stored{k}") for k in range(2)]
        qn_in, qn_std = sem("qn_in"), sem("qn_std")
        rt_in, rt_exp, mask_ready, dest_ready = (sem(k) for k in ("rt_in", "rt_exp", "mask_ready", "dest_ready"))
        ids_stored, ids_loaded, idx_ready = (sem(k) for k in ("ids_stored", "ids_loaded", "idx_ready"))
        xe_loaded = [sem(f"xe_loaded{k}") for k in range(2)]
        hid_ready = sem("hid_ready")
        y_stored = [sem(f"y_stored{k}") for k in range(2)]
        yg_loaded = [sem(f"yg_loaded{k}") for k in range(2)]
        over = [{k: sem(f"over{l}_{k}") for k in
                 ("ix", "w", "x", "xt", "turned", "gu", "act", "hid", "ht", "htt", "down", "y", "stored", "free")} for l in range(DEPTH)]

        def pieces(u):
            t = u.t
            q = slice(t * P, (t + 1) * P)
            found = []

            def put(col, n, lhsT, rhs):
                while n:
                    k = min(n, 512 - col % 512)
                    found.append((col, k, lhsT, rhs(n, k)))
                    col, n = col + k, n - k

            def run(col, n, lhsT, rhs):
                done = [0]

                def cut(left, k):
                    a = rhs[:, done[0]:done[0] + k]
                    done[0] += k
                    return a
                put(col, n, lhsT, cut)

            ext = (t + 1) * P
            if u.kind == "diff":
                for m in range(2):
                    run(512 * m, ext, blk[:, u.h, q], blk[:, 4 + 2 * u.h + m, 0:ext])
                    run(512 * m + t * P, P, identB, aboveB)
            elif u.kind == "fox":
                run(0, ext, blk[:, 16 + u.h, q], blk[:, 20 + u.h, 0:ext])
                run(t * P, P, identB, aboveB)
            elif u.kind == "dsa":
                run(0, ext, blk[:, 14 + u.h // 2, q], KX[:, 1, 0:ext] if u.h % 2 else blk[:, 13, 0:ext])
                if t:
                    run(0, ext, identB, SELt[t])
                else:
                    run(0, P, identB, aboveB)
            else:
                g = u.h // 4
                b = (g // 2) * 4 + u.h % 4
                if u.kind == "ctx":
                    qc = slice((t - XT_TILES) * P, (t - XT_TILES + 1) * P)
                    run(0, CTX, QCTX[:, b, qc], KCTX[:, g, :])
                else:
                    run(0, CTX, QPLAIN[:, b, q], KCTX[:, g, :])
                    lo, n = u.lat[0], len(u.lat)
                    run(CTX, n * P, QROT[:, b, q], KROT[:, g, lo * P:(lo + n) * P])
                    if u.kind == "window":
                        for k, kb in enumerate(u.lat):
                            if kb != t:
                                run(CTX + k * P, P, identB, belowB if kb < t else aboveB)
                if u.l % 3 == 0:
                    run(u.blocks * P, 1, onesF[0:1, 0:P], SINKROW[0:1, u.h:u.h + 1])
            return sorted(found, key=lambda f: f[0] // 512)

        def score_columns(u):
            return u.blocks * P + (1 if u.kind in ("window", "ctx") else 0)

        def values(u):
            if u.kind == "diff":
                return [V1d[:, b, u.h * P:(u.h + 1) * P] for b in range(u.blocks)]
            if u.kind == "fox":
                return [V1f[:, b, u.h * HD:(u.h + 1) * HD] for b in range(u.blocks)]
            if u.kind == "dsa":
                return [V1s[:, b, :] for b in range(u.blocks)]
            g = u.h // 4
            return [V2[:, b, g * HD:(g + 1) * HD] for b in [XT_TILES, XT_TILES + 1] + u.lat]

        SINKROW = small(16)[0:1, :]
        SQS = small(2)
        MASKB = SEL[:, 0:6 * EXPERTS]
        GQK = GSUB[:, 0:2 * HD]

        block = ctx.enter_context(nc.Block())

        def w_ready(eng, u):
            eng.wait_ge(w_loaded[u.slot], 16 * (u.loads))

        w_dram = {
            "w_out": lambda u: ins["w_out"][u.l, :, u.half * 512:(u.half + 1) * 512],
            "w_o": lambda u: ins["w_o_2"][u.l, :, u.half * 512:(u.half + 1) * 512],
            "w_ada": lambda u: ins["w_ada_2"][u.l, :, u.j * 512:(u.j + 1) * 512],
            "w_qkv": lambda u: ins["w_qkv_2"][u.l, :, u.c * 512:(u.c + 1) * 512],
        }

        @block.sync
        def _(sp):
            def free(prev):
                if prev is not None:
                    sp.wait_ge(sc_full if units[prev].kind in ("gate", "up") else pj_full, units[prev].done)

            def load_unit(u):
                free(u.prev)
                tile = slot_tile(u.slot).rearrange("p (c n) -> p c n", c=DC)
                if u.kind == "w_in":
                    o = 0
                    for c0, n in u.cols:
                        d = sp.dma_start(tile[:, :, o:o + n],
                                         ins["w_in"][u.l, :, c0:c0 + n].rearrange("(c p) n -> p c n", p=P))
                        o += n
                        d.then_inc(w_loaded[u.slot], 16)
                else:
                    sp.dma_start(tile, w_dram[u.kind](u).rearrange("(c p) n -> p c n", p=P)).then_inc(
                        w_loaded[u.slot], 16)

            def load_expert(u, e):
                tile = slot_tile(u.slot)
                name = {"gate": "w_gate_2", "up": "w_up_2", "down": "w_down_2"}[u.kind]
                src = ins[name][u.l, bass.ds(e, 1), :, :].rearrange("e k n -> (e k) n")
                c = 4 if u.kind == "down" else DC
                sp.dma_start(tile.rearrange("p (c n) -> p c n", c=c), src.rearrange("(c p) n -> p c n", p=P)).then_inc(
                    w_loaded[u.slot], 16)

            n = 0
            while n < len(units):
                u = units[n]
                if u.kind not in ("gate", "up", "down"):
                    load_unit(u)
                    n += 1
                    continue
                m = units[n:n + 3 * EXPERTS]
                base, l = n, u.l
                for k in range(8):
                    free(m[k].prev)
                    load_expert(m[k], m[k].e)
                with sp.Fori(0, 14) as i:
                    for k in range(8, 14):
                        sp.wait_ge(pj_full if m[k].kind == "down" else sc_full,
                                   i * (4 if m[k].kind == "down" else 2) + m[k - 6].done)
                        load_expert(m[k], i * 2 + m[k].e)
                for k in range(92, 96):
                    free(m[k].prev)
                    load_expert(m[k], m[k].e)
                n += 3 * EXPERTS
                o = over[l]
                sp.wait_ge(idx_ready, l + 1)
                sp.wait_ge(pj_full, m[-1].done)
                count = sp.value_load(OVI[0:1, MAX_OVER:MAX_OVER + 1], min_val=0, max_val=MAX_OVER)
                with sp.Fori(0, MAX_OVER) as j:
                    with sp.If(j < count):
                        e = sp.value_load(OVI[0:1, bass.ds(j, 1)], min_val=0, max_val=EXPERTS - 1)
                        sp.wait_ge(o["down"], j + 1)
                        for k, (name, c) in enumerate((("w_gate_2", DC), ("w_up_2", DC), ("w_down_2", 4))):
                            src = ins[name][l, bass.ds(e, 1), :, :].rearrange("e k n -> (e k) n")
                            sp.dma_start(slot_tile(3 + k).rearrange("p (c n) -> p c n", c=c),
                                         src.rearrange("(c p) n -> p c n", p=P)).then_inc(o["w"], 16)

        @block.tensor
        def _(pe):
            mm, turn = nc.tensor.matmul, nc.tensor.transpose

            def pj_slot(use):
                if use >= 2:
                    pe.wait_ge(pj_free, use - 1)
                return PJ[:, use % 2, :]

            def tr_slot(use):
                if use >= 2:
                    pe.wait_ge(tr_free, use - 1)
                return TR[:, use % 2, :]

            def turn_rows(src, tr, rows=P):
                for g in range(2):
                    bank = tr_slot(tr[g])
                    for k in range(4):
                        c = 4 * g + k
                        m = turn(bank[:, k * P:(k + 1) * P], src[:, c * P:(c + 1) * P], identF)
                    m.then_inc(tr_full, 1)

            def project(dst, xt, t, w, n):
                for c in range(DC):
                    m = mm(dst[:, 0:n], xt[:, c, t * P:(t + 1) * P], w[:, c, 0:n], start=c == 0, stop=c == DC - 1)
                return m

            def unit_tile(u):
                return slot_tile(u.slot).rearrange("p (c n) -> p c n", c=DC)

            pe.wait_ge(consts_loaded, 16 * 4)
            pe.wait_ge(kb_ready, 1)
            for s in steps:
                if s.kind == "open":
                    pe.wait_ge(xs_loaded[s.fin % 2], 16 * s.load)
                    turn_rows(XS[:, (s.fin % 2) * D:(s.fin % 2 + 1) * D], s.tr)
                elif s.kind == "project":
                    w_ready(pe, s.w)
                    if s.t == 0 and s.name == "idx_q":
                        pe.wait_ge(tr_free, s.tr_before)
                    n = sum(c[1] for c in s.w.cols)
                    bank = pj_slot(s.pj)
                    w = unit_tile(s.w)
                    for c in range(DC):
                        m = mm(bank[:, 0:n], XT1[:, c, s.t * P:(s.t + 1) * P], w[:, c, 0:n], start=c == 0,
                               stop=c == DC - 1)
                    m.then_inc(pj_full, 1)
                elif s.kind == "stage_turn":
                    pe.wait_ge(stg_ready, s.stg + 1)
                    bank = tr_slot(s.tr[0])
                    base = (s.stg % 2) * 640
                    for k in range(s.count):
                        m = turn(bank[0:s.rows, k * P:(k + 1) * P], STG[:, base + k * s.rows:base + (k + 1) * s.rows],
                                 identF)
                    m.then_inc(tr_full, 1)
                elif s.kind == "forget":
                    pe.wait_ge(logf_ready, s.l + 1)
                    bank = pj_slot(s.pj)
                    for t in range(XT_TILES):
                        for j in range(t + 1):
                            m = mm(bank[:, 4 * t:4 * t + 4], triF if j == t else onesF, FT[3][:, 4 * j:4 * j + 4],
                                   start=j == 0, stop=j == t)
                    m.then_inc(pj_full, 1)
                elif s.kind == "index":
                    pe.wait_ge(tr_free, s.tr_before)
                    if s.sc >= 2:
                        pe.wait_ge(sc_free, s.sc - 1)
                    ext = (s.t + 1) * P
                    mm(SC[:, s.sc % 2, 0:ext], blk[:, 8 + s.h // 2, s.t * P:(s.t + 1) * P],
                       KX[:, 0, 0:ext] if s.h % 2 else blk[:, 12, 0:ext],
                       start=True, stop=True).then_inc(sc_full, 1)
                elif s.kind == "scores":
                    u = s.u
                    if u.first:
                        pe.wait_ge(tr_free, u.needs)
                        if u.kind in ("window", "ctx"):
                            pe.wait_ge(sink_ready, 1)
                    if u.kind == "dsa" and u.t:
                        pe.wait_ge(topk_done, u.topk)
                    if u.sc >= 2:
                        pe.wait_ge(sc_free, u.sc - 1)
                    ps = pieces(u)
                    for k, (col, n, lhsT, rhs) in enumerate(ps):
                        first = k == 0 or ps[k - 1][0] // 512 != col // 512
                        last = k == len(ps) - 1 or ps[k + 1][0] // 512 != col // 512
                        m = mm(SC[:, u.sc % 2, col:col + n], lhsT, rhs, start=first, stop=last, skip_group_check=True)
                    m.then_inc(sc_full, 1)
                elif s.kind == "turn":
                    u = s.u
                    if u.kind == "diff":
                        pe.wait_ge(mixed_ready, u.mixed)
                    else:
                        pe.wait_ge(sc_free, u.sc + 1)
                    base = (u.index % 2) * 1024
                    for k, use in enumerate(u.tr):
                        bank = tr_slot(use)
                        for b in range(4 * k, min(4 * k + 4, u.blocks)):
                            m = turn(bank[:, (b - 4 * k) * P:(b - 4 * k + 1) * P], PR[:, base + b * P:base + (b + 1) * P],
                                     identF)
                        m.then_inc(tr_full, 1)
                elif s.kind == "weigh":
                    u = s.u
                    pe.wait_ge(tr_free, u.tr[-1] + 1)
                    bank = pj_slot(u.pj)
                    vs = values(u)
                    n = P if u.kind == "diff" else HD
                    for b, v in enumerate(vs):
                        for r in range(0, P, HALF_ROWS):
                            o = (u.index % 2) * 768 + b * P + r
                            m = mm(bank[r:r + HALF_ROWS, 0:n], PT[:, o:o + HALF_ROWS], v, start=b == 0,
                                   stop=b == len(vs) - 1)
                    m.then_inc(pj_full, 1)
                elif s.kind == "ada":
                    w_ready(pe, s.w)
                    pe.wait_ge(c_silu, 1)
                    bank = pj_slot(s.pj)
                    w = unit_tile(s.w)
                    for c in range(DC):
                        for g in range(4):
                            m = mm(bank[32 * g:32 * g + 2, 0:P], SCT[:, 2 * c:2 * c + 2], w[:, c, g * P:(g + 1) * P],
                                   start=c == 0, stop=c == DC - 1)
                    m.then_inc(pj_full, 1)
                elif s.kind == "mix_turn":
                    pe.wait_ge(sub_done, XT_TILES * s.l + s.t + 1)
                    turn_rows(G1[:, s.t], s.tr)
                elif s.kind in ("wout", "wo"):
                    pe.wait_ge(tr_free, s.src_tr + 1)
                    xt = XT1 if s.kind == "wout" else XT2
                    for h in range(2):
                        w_ready(pe, s.w[h])
                        project(pj_slot(s.pj[h]), xt, s.t, unit_tile(s.w[h]), 512).then_inc(pj_full, 1)
                elif s.kind == "fin_turn":
                    f = s.f
                    pe.wait_ge(fin_done, f.q)
                    k = f.fin % 2
                    turn_rows(HS[:, k] if f.normed else XS[:, k * D:(k + 1) * D], s.tr)
                elif s.kind == "qkv":
                    w_ready(pe, s.w)
                    if s.c in (0, 2) and s.t in (0, XT_TILES):
                        pe.wait_ge(tr_free, s.tr_before)
                    project(pj_slot(s.pj), XT2, s.t, unit_tile(s.w), 512).then_inc(pj_full, 1)
                elif s.kind == "qk_turn":
                    q = s.s
                    for k, use in enumerate(s.tr):
                        pe.wait_ge(stg_ready, q.stg[k] + 1)
                        bank = tr_slot(use)
                        base = (q.stg[k] % 2) * 640
                        for b in range(4 if q.c < 2 else 2):
                            m = turn(bank[:, b * P:(b + 1) * P], STG[:, base + b * P:base + (b + 1) * P], identF)
                        m.then_inc(tr_full, 1)
                elif s.kind == "o_turn":
                    pe.wait_ge(pj_free, s.after + 1)
                    turn_rows(O2[:, s.t % 2], s.tr)
                elif s.kind == "route":
                    pe.wait_ge(router_loaded, 16 * 4 * (s.l + 1))
                    pe.wait_ge(tr_free, s.tr_before)
                    bank = pj_slot(s.pj[0])
                    for t in range(s.tiles):
                        dst = bank[:, t * ROUTER:(t + 1) * ROUTER]
                        for r in range(0, P, HALF_ROWS):
                            mm(dst[r:r + HALF_ROWS], onesF[0:1, 0:HALF_ROWS], RB[0:1, :], start=True, stop=False)
                        for c in range(DC):
                            for r in range(0, P, HALF_ROWS):
                                m = mm(dst[r:r + HALF_ROWS], XT2[:, c, t * P + r:t * P + r + HALF_ROWS],
                                       RWT[:, c * ROUTER:(c + 1) * ROUTER], start=False, stop=c == DC - 1)
                    m.then_inc(pj_full, 1)
                    bank = pj_slot(s.pj[1])
                    pe.wait_ge(mask_ready, s.l + 1)
                    for t in range(s.tiles):
                        for j in range(t + 1):
                            mm(bank[:, t * EXPERTS:(t + 1) * EXPERTS], beforeB if j == t else onesB,
                               MASKB[:, j * EXPERTS:(j + 1) * EXPERTS], start=j == 0, stop=j == t)
                    for j in range(s.tiles):
                        m = mm(bank[:, s.tiles * EXPERTS:(s.tiles + 1) * EXPERTS], onesB,
                               MASKB[:, j * EXPERTS:(j + 1) * EXPERTS], start=j == 0, stop=j == s.tiles - 1)
                    m.then_inc(pj_full, 1)
                    bank = pj_slot(s.pj[2])
                    pe.wait_ge(ids_loaded, 16 * (s.l + 1))
                    turn(bank[:, 0:BLOCKS], STG[0:BLOCKS, 0:P], identF[0:BLOCKS, 0:BLOCKS]).then_inc(pj_full, 1)
                elif s.kind == "moe":
                    T0, S0, J0 = s.tr[0], s.sc[0], s.pj[0]
                    m = units[s.base:s.base + 3 * EXPERTS]
                    down_unit = {u.e: u for u in m if u.kind == "down"}
                    gate_unit = {u.e: u for u in m if u.kind == "gate"}
                    up_unit = {u.e: u for u in m if u.kind == "up"}

                    def turn_x(at_, r):
                        par = r % 2
                        pe.wait_ge(xe_loaded[par], at_(16, 16 * (r // 2 + 1) + s.xe0[par]))
                        for g in range(2):
                            use = T0 + (3 * r - 1 + g if r else g)
                            pe.wait_ge(tr_free, at_(6, use - 1))
                            for k in range(4):
                                c = 4 * g + k
                                x = turn(TR[:, use % 2, k * P:(k + 1) * P], XE[par][:, c * P:(c + 1) * P], identF)
                            x.then_inc(tr_full, 1)

                    def gate_up(at_, r):
                        par = r % 2
                        bank = SC[:, (S0 + r) % 2, :]
                        pe.wait_ge(tr_free, at_(6, T0 + (3 * r if r else 1) + 1))
                        pe.wait_ge(sc_free, at_(2, S0 + r - 1))
                        for k, u in enumerate((gate_unit[r], up_unit[r])):
                            pe.wait_ge(w_loaded[u.slot], at_(16, 16 * u.loads))
                            w = unit_tile(u)
                            for c in range(DC):
                                x = mm(bank[:, k * 512:(k + 1) * 512], XET[par][:, c, :], w[:, c, :], start=c == 0,
                                       stop=c == DC - 1)
                        x.then_inc(sc_full, 1)

                    def turn_hidden(at_, r):
                        use = T0 + 4 + 3 * r
                        pe.wait_ge(hid_ready, at_(2, s.l * EXPERTS + r + 1))
                        pe.wait_ge(tr_free, at_(6, use - 1))
                        for k in range(4):
                            x = turn(TR[:, use % 2, k * P:(k + 1) * P], HID[r % 2][:, k * P:(k + 1) * P], identF)
                        x.then_inc(tr_full, 1)

                    def down(at_, r):
                        u = down_unit[r]
                        pe.wait_ge(w_loaded[u.slot], at_(16, 16 * u.loads))
                        pe.wait_ge(tr_free, at_(6, T0 + 4 + 3 * r + 1))
                        w = slot_tile(u.slot).rearrange("p (c n) -> p c n", c=4)
                        for h in range(2):
                            use = J0 + 2 * r + h
                            pe.wait_ge(pj_free, at_(4, use - 1))
                            for c in range(4):
                                x = mm(PJ[:, use % 2, :], HTD[r % 2][:, c, :], w[:, c, h * 512:(h + 1) * 512],
                                       start=c == 0, stop=c == 3)
                            x.then_inc(pj_full, 1)

                    def step(at_, r, ahead=True):
                        if ahead:
                            gate_up(at_, r + 1)
                        turn_hidden(at_, r)
                        if ahead:
                            turn_x(at_, r + 2)
                        down(at_, r)

                    once = lambda a, b: b
                    turn_x(once, 0)
                    turn_x(once, 1)
                    gate_up(once, 0)
                    step(once, 0)
                    with pe.Fori(0, EXPERTS // 2 - 1) as i:
                        for r in (1, 2):
                            step(lambda a, b: i * a + b, r)
                    step(once, EXPERTS - 1, ahead=False)

                    o = over[s.l]
                    pe.wait_ge(tr_free, s.tr[-1] + 1)
                    pe.wait_ge(pj_free, s.pj[-1] + 1)
                    pe.wait_ge(sc_free, s.sc[-1] + 1)
                    count = pe.value_load(OVI[0:1, MAX_OVER:MAX_OVER + 1], min_val=0, max_val=MAX_OVER)
                    with pe.Fori(0, MAX_OVER) as j:
                        with pe.If(j < count):
                            pe.wait_ge(o["x"], j * 16 + 16)
                            for g in range(2):
                                for k in range(4):
                                    c = 4 * g + k
                                    x = turn(TR[:, g, k * P:(k + 1) * P], XE[0][:, c * P:(c + 1) * P], identF)
                            x.then_inc(o["turned"], 1)
                            pe.wait_ge(o["xt"], j + 1)
                            pe.wait_ge(o["w"], j * 48 + 48)
                            for k in range(2):
                                w = slot_tile(3 + k).rearrange("p (c n) -> p c n", c=DC)
                                for c in range(DC):
                                    x = mm(SC[:, 0, k * 512:(k + 1) * 512], XET[0][:, c, :], w[:, c, :], start=c == 0,
                                           stop=c == DC - 1)
                            x.then_inc(o["gu"], 1)
                            pe.wait_ge(o["hid"], j + 1)
                            for k in range(4):
                                x = turn(TR[:, 0, k * P:(k + 1) * P], HID[0][:, k * P:(k + 1) * P], identF)
                            x.then_inc(o["ht"], 1)
                            pe.wait_ge(o["htt"], j + 1)
                            w = slot_tile(5).rearrange("p (c n) -> p c n", c=4)
                            for h in range(2):
                                for c in range(4):
                                    x = mm(PJ[:, h, :], HTD[0][:, c, :], w[:, c, h * 512:(h + 1) * 512], start=c == 0,
                                           stop=c == 3)
                            x.then_inc(o["down"], 1)
                            pe.wait_ge(o["y"], j + 1)

        @block.scalar
        def _(act):
            a = Counting()
            A = a.of(nc.scalar.activation)

            def copy(dst, src):
                return A(dst, src, ACT.Copy)

            def to_xt(xt, t, tr):
                for g in range(2):
                    act.wait_ge(tr_full, tr[g] + 1)
                    copy(xt[:, 4 * g:4 * g + 4, t * P:(t + 1) * P],
                         TR[:, tr[g] % 2, :].rearrange("p (c n) -> p c n", c=4)).then_inc(tr_free, 1)

            act.wait_ge(c_loaded, 32)
            A(SCT, SCR, ACT.Silu).then_inc(c_silu, 1)
            two_before = {}
            for s in steps:
                act.wait_ge(*a.latest)
                if s.kind == "open":
                    to_xt(XT1, s.t, s.tr)
                elif s.kind == "fin_turn":
                    to_xt(XT1 if s.f.kind == "wout" else XT2, s.f.t, s.tr)
                elif s.kind == "mix_turn":
                    to_xt(XT1, s.t, s.tr)
                elif s.kind == "o_turn":
                    to_xt(XT2, s.t, s.tr)
                elif s.kind == "layer1":
                    act.wait_ge(lam_in, s.l + 1)
                    A(LAMS[:, 2:4], LAMS[:, 0:2], ACT.Exp).then_inc(lam_exp, 1)
                elif s.kind == "stage_turn":
                    act.wait_ge(tr_full, s.tr[0] + 1)
                    t = s.s.t
                    src = TR[0:s.rows, s.tr[0] % 2, 0:s.count * P].rearrange("p (c n) -> p c n", n=P)
                    c = slice(t * P, (t + 1) * P)
                    if s.block == 4:
                        halves = blk[:, 4:12, c].rearrange("p (h m) n -> p h m n", m=2)
                        copy(halves[0:HD, :, 0], src[0:HD])
                        x = copy(halves[HD:P, :, 1], src[HD:P])
                    elif s.block in (12, 13):
                        copy(blk[0:HD, s.block, c], src[0:HD, 0])
                        x = copy(KX[HD:P, s.block - 12, c], src[HD:P, 0])
                        if s.count > 1:
                            x = copy(blk[:, s.block + 1:s.block + s.count, c], src[:, 1:])
                    else:
                        x = copy(blk[0:s.rows, s.block:s.block + s.count, c], src)
                    x.then_inc(tr_free, 1)
                elif s.kind == "log_f":
                    act.wait_ge(fox_in, s.l + 1)
                    A(FT[1], FT[0], ACT.Exp).then_inc(fox_exp, 1)
                    act.wait_ge(fox_one, s.l + 1)
                    A(FT[2], FT[1], ACT.Ln).then_inc(fox_ln, 1)
                elif s.kind == "project" and s.name in ("gate0", "gate1"):
                    g = G1[:, s.t, 512 * (s.name == "gate1"):512 * (s.name == "gate1") + 512]
                    act.wait_ge(gate_raw, s.gate)
                    A(g, g, ACT.Silu).then_inc(gate_ready, 1)
                elif s.kind == "index":
                    act.wait_ge(sc_full, s.sc + 1)
                    if s.index >= 2:
                        act.wait_ge(rel_used, s.index - 1)
                    ext = (s.t + 1) * P
                    A(REL[s.index % 2][:, 0:ext], SC[:, s.sc % 2, 0:ext], ACT.Relu).then_inc(sc_free, 1)
                elif s.kind == "scores":
                    u = s.u
                    act.wait_ge(nm_ready, u.index + 1)
                    if u.index >= 2:
                        act.wait_ge(tr_full, two_before[u.index - 2].tr[-1] + 1)
                    two_before[u.index] = u
                    k = 2 * (u.index % 4)
                    base = (u.index % 2) * 1024
                    n = score_columns(u)
                    for m in range(2 if u.kind == "diff" else 1):
                        x = A(PR[:, base + 512 * m:base + 512 * m + n], SC[:, u.sc % 2, 512 * m:512 * m + n], ACT.Exp,
                              bias=NM[:, k + m:k + m + 1], scale=-1.0, accum_out=LS[:, k + m:k + m + 1])
                    x.then_inc(sc_free, 1)
                elif s.kind == "turn":
                    u = s.u
                    if u.index >= 2:
                        act.wait_ge(pj_full, two_before[u.index - 2].pj + 1)
                    if u.kind == "diff":
                        act.wait_ge(rel_used, 24 * (u.l + 1))
                    for k, use in enumerate(u.tr):
                        n = min(4, u.blocks - 4 * k) * P
                        act.wait_ge(tr_full, use + 1)
                        o = (u.index % 2) * 768 + 512 * k
                        copy(PT[:, o:o + n], TR[:, use % 2, 0:n]).then_inc(tr_free, 1)
                elif s.kind == "subln":
                    act.wait_ge(sub_in, s.l + 1)
                    A(RS, SS, ACT.Sqrt).then_inc(sub_out, 1)
                elif s.kind == "wout":
                    k = s.fin % 2
                    act.wait_ge(std_in, s.sd)
                    A(STD[:, k:k + 1], AGG[:, 2 * k + 1:2 * k + 2], ACT.Sqrt, bias=EPS[:, 0:1]).then_inc(std_ready, 1)
                elif s.kind in ("norm0", "wo", "combine"):
                    k = s.fin % 2
                    if s.kind == "norm0":
                        act.wait_ge(xs_loaded[k], 16 * s.load)
                        act.wait_ge(fin_done, s.q - 1)
                    else:
                        act.wait_ge(std_in, s.sd)
                    A(JUNK, XS[:, k * D:(k + 1) * D], ACT.Square, accum_out=SQS[:, k:k + 1]).then_inc(act_done, 1)
                    act.wait_ge(act_done, s.normn)
                    A(STD[:, k:k + 1], SQS[:, k:k + 1], ACT.Sqrt, scale=1.0 / D, bias=EPS[:, 1:2]).then_inc(std_ready, 1)
                elif s.kind == "qkv" and s.l % 3 == 1:
                    act.wait_ge(qn_in, s.qn)
                    n = 8 if s.c < 2 else 4
                    A(QN[:, 16:16 + n], QN[:, 8:8 + n], ACT.Sqrt, bias=EPS[:, 1:2]).then_inc(qn_std, 1)
                elif s.kind == "qk_turn":
                    q = s.s
                    for k, use in enumerate(s.tr):
                        act.wait_ge(tr_full, use + 1)
                        nb = 4 if q.c < 2 else 2
                        c = slice((q.t % XT_TILES) * P, (q.t % XT_TILES + 1) * P)
                        src = TR[:, use % 2, 0:nb * P].rearrange("p (c n) -> p c n", n=P)
                        if q.c < 2:
                            dst = (QCTX if q.t >= XT_TILES else (QPLAIN, QROT)[k])[:, 4 * q.c:4 * q.c + 4]
                            x = copy(dst[:, :, c], src)
                        else:
                            dst = (KCTX if q.t >= XT_TILES else KROT)[:, :, c].rearrange("p (j m) n -> p j m n", m=2)
                            copy(dst[0:HD, :, 0], src[0:HD])
                            x = copy(dst[HD:P, :, 1], src[HD:P])
                        x.then_inc(tr_free, 1)
                elif s.kind == "route":
                    n = s.tiles * GROUPS
                    act.wait_ge(rt_in, 2 * s.l + 1)
                    A(RT["ge"][:, 0:n], RT["ge"][:, 0:n], ACT.Exp).then_inc(rt_exp, 1)
                    act.wait_ge(rt_in, 2 * s.l + 2)
                    A(RT["e2"][:, 0:s.tiles], RT["e2"][:, 0:s.tiles], ACT.Exp).then_inc(rt_exp, 1)
                elif s.kind == "moe":
                    T0, S0, J0 = s.tr[0], s.sc[0], s.pj[0]

                    def x_in(at_, r):
                        for g in range(2):
                            use = T0 + (3 * r - 1 + g if r else g)
                            act.wait_ge(tr_full, at_(6, use + 1))
                            if r >= 2:
                                act.wait_ge(sc_full, at_(2, S0 + r - 1))
                            copy(XET[r % 2][:, 4 * g:4 * g + 4, :],
                                 TR[:, use % 2, :].rearrange("p (c n) -> p c n", c=4)).then_inc(tr_free, 1)

                    def hidden(at_, r):
                        bank = SC[:, (S0 + r) % 2, :]
                        act.wait_ge(sc_full, at_(2, S0 + r + 1))
                        if r >= 2:
                            act.wait_ge(hid_ready, at_(2, s.l * EXPERTS + r - 1))
                        A(GSI[r % 2], bank[:, 0:512], ACT.Silu)
                        copy(UPS[r % 2], bank[:, 512:1024]).then_inc(sc_free, 1)

                    def hidden_turned(at_, r):
                        use = T0 + 4 + 3 * r
                        act.wait_ge(tr_full, at_(6, use + 1))
                        act.wait_ge(pj_full, at_(4, J0 + 2 * r - 2))
                        copy(HTD[r % 2], TR[:, use % 2, :].rearrange("p (c n) -> p c n", c=4)).then_inc(tr_free, 1)

                    once = lambda a, b: b
                    x_in(once, 0)
                    x_in(once, 1)
                    hidden(once, 0)
                    hidden_turned(once, 0)
                    x_in(once, 2)
                    hidden(once, 1)
                    with act.Fori(0, EXPERTS // 2 - 1) as i:
                        for r in (1, 2):
                            lin = lambda a, b: i * a + b
                            hidden_turned(lin, r)
                            x_in(lin, r + 2)
                            hidden(lin, r + 1)
                    hidden_turned(once, EXPERTS - 1)
                    a.count[tr_free.name] += 6 * (EXPERTS // 2 - 2)
                    a.count[sc_free.name] += 2 * (EXPERTS // 2 - 2)
                    a.latest = (tr_free, a.count[tr_free.name])
                    o = over[s.l]
                    act.wait_ge(idx_ready, s.l + 1)
                    count = act.value_load(OVI[0:1, MAX_OVER:MAX_OVER + 1], min_val=0, max_val=MAX_OVER)
                    with act.Fori(0, MAX_OVER) as j:
                        with act.If(j < count):
                            act.wait_ge(o["turned"], j + 2)
                            for g in range(2):
                                x = copy(XET[0][:, 4 * g:4 * g + 4, :],
                                         TR[:, g, :].rearrange("p (c n) -> p c n", c=4))
                            x.then_inc(o["xt"], 1)
                            act.wait_ge(o["gu"], j + 1)
                            A(GSI[0], SC[:, 0, 0:512], ACT.Silu)
                            copy(UPS[0], SC[:, 0, 512:1024]).then_inc(o["act"], 1)
                            act.wait_ge(o["ht"], j + 1)
                            copy(HTD[0], TR[:, 0, :].rearrange("p (c n) -> p c n", c=4)).then_inc(o["htt"], 1)
                    a.latest = (tr_free, a.count[tr_free.name])

        @block.vector
        def _(dve):
            e = nc.vector
            v = Counting()
            tensor_copy, memset, reciprocal, tensor_reduce = (v.of(k) for k in (e.tensor_copy, e.memset, e.reciprocal,
                                                                                e.tensor_reduce))
            bn_stats, bn_aggr, match_replace, top8 = (v.of(k) for k in (e.bn_stats, e.bn_aggr, e.match_replace, e.max))
            scan, multiply_reduce = v.of(e.tensor_tensor_scan), v.of(e.tensor_tensor_reduce)
            TT, TS, STT = v.of(e.tensor_tensor), v.of(e.tensor_scalar), v.of(e.scalar_tensor_tensor)

            def now(x):
                x.then_inc(dve_done, 1)
                settle()

            def mark(x):
                x.then_inc(dve_done, 1)

            def settle():
                dve.wait_ge(*v.latest)

            def rotate(src, dst, heads, t, scale, pair, release=None):
                n = heads * HD
                a, b = TMP[:, 0:n], TMP[:, 512:512 + n]
                cos = ropeC[:, t, :].unsqueeze(1).to_broadcast([P, heads, HD])
                src3 = src.rearrange("p (h d) -> p h d", d=HD)
                if pair == 32:
                    STT(a.rearrange("p (h d) -> p h d", d=HD), src3, scale, cos, ALU.mult, ALU.mult)
                    b3 = b.rearrange("p (h d) -> p h d", d=HD)
                    for k in range(2):
                        sin = ropeS[:, t, 32 * k:32 * k + 32].unsqueeze(1).to_broadcast([P, heads, 32])
                        x = STT(b3[:, :, 32 * k:32 * k + 32], src3[:, :, 32 - 32 * k:64 - 32 * k], scale, sin, ALU.mult,
                                ALU.mult)
                else:
                    TT(a.rearrange("p (h d) -> p h d", d=HD), src3, cos, ALU.mult)
                    for f in range(2):
                        b4 = b.rearrange("p (h f d) -> p h f d", f=2, d=32)[:, :, f, :]
                        s4 = src.rearrange("p (h f d) -> p h f d", f=2, d=32)[:, :, f, :]
                        for k in range(2):
                            sin = ropeS[:, t, 32 * f + 16 * k:32 * f + 16 * k + 16].unsqueeze(1).to_broadcast([P, heads, 16])
                            x = TT(b4[:, :, 16 * k:16 * k + 16], s4[:, :, 16 - 16 * k:32 - 16 * k], sin, ALU.mult)
                x.then_inc(dve_done if release is None else release, 1)
                settle()
                return TT(dst, a, b, ALU.add)

            dve.wait_ge(consts_loaded, 64)
            for dst, src in ((identB, identF), (aboveB, aboveF), (belowB, G[:, 0:P]), (beforeB, G[:, P:2 * P])):
                tensor_copy(dst, src)
            memset(EPS[:, 0:1], EPS1)
            memset(EPS[:, 1:2], EPS2)
            tensor_copy(onesB, onesF).then_inc(kb_ready, 1)
            memset(BC[:, 0:D], 0.0)
            memset(KX[0:HD], 0.0)
            memset(blk[HD:P, 12:14], 0.0)
            mark(memset(blk[HD:P, 16:24], 0.0))
            settle()
            memset(G[0:BLOCKS, 2 * P:3 * P], 0.0).then_inc(zeros_ready, 1)

            def stage(use):
                if use >= 2:
                    dve.wait_ge(tr_full, turned_by[use - 2] + 1)
                return (use % 2) * 640

            def finish_norm(s):
                k = s.fin % 2
                x = XS[:, k * D:(k + 1) * D]
                dve.wait_ge(std_ready, s.q)
                now(reciprocal(RSTD[:, k:k + 1], STD[:, k:k + 1]))
                dve.wait_ge(bc_loaded, 16 * s.bc_dmas)
                prev = by_fin.get(s.fin - 2)
                if prev is not None and prev.normed:
                    if prev.turned is not None:
                        dve.wait_ge(tr_full, prev.turned + 1)
                    if prev.stores_h:
                        dve.wait_ge(h_stored[k], 16 * prev.hst[k])
                y = STT(HS[:, k], x, RSTD[:, k:k + 1], BC[:, 0:D], ALU.mult, ALU.mult)
                if s.kind == "combine" and s.last:
                    y.then_inc(fin_done, 1)
                else:
                    now(y)
                    TT(HS[:, k], HS[:, k], BC[:, D:2 * D], ALU.add).then_inc(fin_done, 1)

            for s in steps:
                settle()
                if s.kind == "layer1":
                    lam_init = 0.8 - 0.6 * math.exp(-0.3 * s.l)
                    dve.wait_ge(layer_loaded, 16 * s.loaded)
                    for k in range(2):
                        now(TT(LAMV[:, 128 * k:128 * k + 64], LAMV[:, 128 * k:128 * k + 64],
                               LAMV[:, 128 * k + 64:128 * k + 128], ALU.mult))
                        x = tensor_reduce(LAMS[:, k:k + 1], LAMV[:, 128 * k:128 * k + 64], AX.X, ALU.add)
                        if k == 1:
                            x.then_inc(lam_in, 1)
                    dve.wait_ge(lam_exp, s.l + 1)
                    now(TT(NLAM, LAMS[:, 3:4], LAMS[:, 2:3], ALU.subtract))
                    now(TS(NLAM, NLAM, -lam_init, None, ALU.add))
                elif s.kind == "project":
                    dve.wait_ge(pj_full, s.pj + 1)
                    bank = PJ[:, s.pj % 2, :]
                    t = s.t
                    base = stage(s.stg[0]) if s.stg else None
                    if s.name == "diff_k" and t == 0:
                        halves = blk[:, 4:12].rearrange("p (h m) n -> p h m n", m=2)
                        memset(halves[HD:P, :, 0], 0.0)
                        now(memset(halves[0:HD, :, 1], 0.0))
                    if s.name in ("idx_q", "diff_q", "diff_k"):
                        rotate(bank, STG[:, base:base + 512], 8, t, -SCALE if s.name == "diff_q" else 1.0, 32,
                               pj_free).then_inc(stg_ready, 1)
                    elif s.name == "idx_k":
                        TS(WIDX[:, 8 * t:8 * t + 8], bank[:, 64:72], IDX_SCALE, None, ALU.mult)
                        TT(FFZ[:, 4 * t:4 * t + 4], bank[:, 72:76], BFT, ALU.add)
                        tensor_copy(V1f[:, t], bank[:, 76:332])
                        now(rotate(bank[:, 0:64], STG[:, base:base + 64], 1, t, 1.0, 32, pj_free))
                        tensor_copy(STG[:, base + 64:base + 128], STG[:, base:base + 64]).then_inc(stg_ready, 1)
                    elif s.name == "dsa":
                        tensor_copy(V1s[:, t], bank[:, 320:384])
                        now(rotate(bank[:, 0:256], STG[:, base + 128:base + 384], 4, t, -SCALE, 32))
                        now(rotate(bank[:, 256:320], STG[:, base:base + 64], 1, t, 1.0, 32, pj_free))
                        tensor_copy(STG[:, base + 64:base + 128], STG[:, base:base + 64]).then_inc(stg_ready, 1)
                    elif s.name == "fox":
                        q = STG[:, base:base + 264].rearrange("p (h n) -> p h n", h=4)
                        cum = CUM[:, 4 * t:4 * t + 4].unsqueeze(2)
                        one = onesF[:, 0:4].unsqueeze(2)
                        TS(q[:, :, 0:64], bank[:, 0:256].rearrange("p (h n) -> p h n", h=4), -SCALE, None, ALU.mult)
                        tensor_copy(q[:, :, 64:65], one)
                        TS(q[:, :, 65:66], cum, -1.0, None, ALU.mult).then_inc(stg_ready, 1)
                        base = stage(s.stg[1])
                        k = STG[:, base:base + 264].rearrange("p (h n) -> p h n", h=4)
                        tensor_copy(k[:, :, 0:64], bank[:, 256:512].rearrange("p (h n) -> p h n", h=4)).then_inc(pj_free, 1)
                        tensor_copy(k[:, :, 64:65], cum)
                        tensor_copy(k[:, :, 65:66], one).then_inc(stg_ready, 1)
                    elif s.name == "diff_v":
                        tensor_copy(V1d[:, t], bank).then_inc(pj_free, 1)
                    else:
                        if s.l == 0:
                            dve.wait_ge(idt_zeroed, 16)
                        g = 512 * (s.name == "gate1")
                        tensor_copy(G1[:, t, g:g + 512], bank).then_inc(pj_free, 1)
                        settle()
                        v.increment(dve, gate_raw, 1)
                elif s.kind == "log_f":
                    now(tensor_copy(FT[0], FFZ))
                    STT(FT[0], FFZ, -1.0, FFZ, ALU.mult, ALU.min).then_inc(fox_in, 1)
                    dve.wait_ge(fox_exp, s.l + 1)
                    TS(FT[1], FT[1], 1.0, None, ALU.add).then_inc(fox_one, 1)
                    dve.wait_ge(fox_ln, s.l + 1)
                    STT(FT[3], FFZ, 0.0, FT[2], ALU.min, ALU.subtract).then_inc(logf_ready, 1)
                elif s.kind == "forget":
                    dve.wait_ge(pj_full, s.pj + 1)
                    tensor_copy(CUM, PJ[:, s.pj % 2, 0:16]).then_inc(pj_free, 1)
                    settle()
                elif s.kind == "index":
                    dve.wait_ge(sc_free, s.sc + 1)
                    ext = (s.t + 1) * P
                    w = WIDX[:, 8 * s.t + s.h:8 * s.t + s.h + 1]
                    r, acc = REL[s.index % 2][:, 0:ext], Wk[s.t]
                    if s.index == 0:
                        dve.wait_ge(yd_zeroed, 16 * MAX_OVER)
                    if s.h == 0:
                        TS(acc, r, w, None, ALU.mult).then_inc(rel_used, 1)
                    else:
                        dve.wait_ge(rel_used, s.index)
                        STT(acc, r, w, acc, ALU.mult, ALU.add).then_inc(rel_used, 1)
                    if s.h == IDX_HEADS - 1:
                        dve.wait_ge(rel_used, s.index + 1)
                        now(TT(acc[:, ext - P:ext], acc[:, ext - P:ext], aboveF, ALU.subtract))
                elif s.kind == "topk":
                    for _ in range(s.rounds):
                        now(top8(M8, Wk[s.t]))
                        now(match_replace(Wk[s.t], M8, Wk[s.t], REPLACED))
                    if s.last:
                        TS(SELt[s.t], Wk[s.t], REPLACED / 2, BIG, ALU.is_gt, ALU.mult).then_inc(topk_done, 1)
                elif s.kind == "scores":
                    u = s.u
                    dve.wait_ge(sc_full, u.sc + 1)
                    k = 2 * (u.index % 4)
                    if u.kind == "diff":
                        tensor_reduce(NM[:, k:k + 2], SC[:, u.sc % 2, :].rearrange("p (m n) -> p m n", m=2)[:, :, 0:u.blocks * P],
                                        AX.X, ALU.min).then_inc(nm_ready, 1)
                    else:
                        tensor_reduce(NM[:, k:k + 1], SC[:, u.sc % 2, 0:score_columns(u)], AX.X, ALU.min).then_inc(nm_ready, 1)
                elif s.kind == "turn":
                    u = s.u
                    if u.kind == "diff":
                        dve.wait_ge(sc_free, u.sc + 1)
                        k = 2 * (u.index % 4)
                        base = (u.index % 2) * 1024
                        n = u.blocks * P
                        now(reciprocal(RI[:, k:k + 2], LS[:, k:k + 2]))
                        now(STT(CC[:, 0:1], RI[:, k + 1:k + 2], NLAM, LS[:, k:k + 1], ALU.mult, ALU.mult))
                        STT(PR[:, base:base + n], PR[:, base + 512:base + 512 + n], CC[:, 0:1], PR[:, base:base + n], ALU.mult,
                            ALU.add).then_inc(mixed_ready, 1)
                elif s.kind == "weigh":
                    u = s.u
                    t = u.t
                    dve.wait_ge(pj_full, u.pj + 1)
                    k = 2 * (u.index % 4)
                    bank = PJ[:, u.pj % 2, :]
                    if u.kind != "diff":
                        now(reciprocal(RI[:, k:k + 1], LS[:, k:k + 1]))
                    ri = RI[:, k:k + 1]
                    if u.kind == "diff":
                        a = ARAW[:, (4 * t + u.h) * P:(4 * t + u.h + 1) * P]
                        TS(a, bank[:, 0:P], ri, None, ALU.mult).then_inc(pj_free, 1)
                        settle()
                        mark(multiply_reduce(out=TMP[:, 0:P], in0=a, in1=a, scale=1.0, scalar=0.0, op0=ALU.mult,
                                                    op1=ALU.add, accum_out=SS[:, 4 * t + u.h:4 * t + u.h + 1]))
                    elif u.kind in ("fox", "dsa"):
                        c = (768 if u.kind == "fox" else 512) + HD * u.h
                        dve.wait_ge(gate_ready, 8 * (u.l + 1))
                        STT(G1[:, t, c:c + HD], bank[:, 0:HD], ri, G1[:, t, c:c + HD], ALU.mult, ALU.mult).then_inc(pj_free, 1)
                    else:
                        if u.h == 0 and u.o_before is not None:
                            dve.wait_ge(tr_full, u.o_before + 1)
                        TS(O2[:, t % 2, u.h * HD:(u.h + 1) * HD], bank[:, 0:HD], ri, None, ALU.mult).then_inc(pj_free, 1)
                elif s.kind == "ada":
                    k = s.ada % 2
                    o = k * D
                    dve.wait_ge(pj_full, s.pj + 1)
                    dve.wait_ge(ada_loaded[k], 16 * s.ada_dmas)
                    for g in range(4):
                        r = slice(32 * g, 32 * g + 2)
                        x = TT(XS[r, o:o + P], PJ[r, s.pj % 2, 0:P], XS[r, o:o + P], ALU.add)
                    x.then_inc(pj_free, 1)
                    settle()
                    if s.j // 2 in (1, 4):
                        for g in range(4):
                            r = slice(32 * g, 32 * g + 2)
                            x = STT(XS[r, o:o + P], XS[r, o:o + P], 1.0, XS[r, o + P:o + 2 * P], ALU.add, ALU.mult)
                        x.then_inc(ada_ready, 1)
                    else:
                        v.increment(dve, ada_ready, 1)
                elif s.kind == "subln":
                    lam_init = 0.8 - 0.6 * math.exp(-0.3 * s.l)
                    now(TS(SS, SS, 1.0 / P, EPS1, ALU.mult, ALU.add))
                    v.increment(dve, sub_in, 1)
                    dve.wait_ge(sub_out, s.l + 1)
                    now(reciprocal(RS, RS))
                    now(TS(RS, RS, 1.0 - lam_init, None, ALU.mult))
                    for t in range(XT_TILES):
                        for h in range(4):
                            a = ARAW[:, (4 * t + h) * P:(4 * t + h + 1) * P]
                            x = STT(a, a, RS[:, 4 * t + h:4 * t + h + 1], GSUB, ALU.mult, ALU.mult)
                        now(x)
                        TT(G1[:, t, 0:512], G1[:, t, 0:512], ARAW[:, 512 * t:512 * t + 512], ALU.mult).then_inc(sub_done, 1)
                elif s.kind == "wout":
                    k = s.fin % 2
                    x = XS[:, k * D:(k + 1) * D]
                    dve.wait_ge(xs_loaded[k], 16 * s.load)
                    for h in range(2):
                        dve.wait_ge(pj_full, s.pj[h] + 1)
                        xh = x[:, 512 * h:512 * h + 512]
                        STT(xh, xh, ALPHA, PJ[:, s.pj[h] % 2, :], ALU.mult, ALU.add).then_inc(pj_free, 1)
                        settle()
                        y = bn_stats(STATS[:, 12 * k + 6 * h:12 * k + 6 * h + 6], xh)
                    now(y)
                    now(bn_aggr(AGG[:, 2 * k:2 * k + 2], STATS[:, 12 * k:12 * k + 12]))
                    v.increment(dve, std_in, 1)
                    dve.wait_ge(std_ready, s.q)
                    now(reciprocal(RSTD[:, k:k + 1], STD[:, k:k + 1]))
                    now(TS(x, x, AGG[:, 2 * k:2 * k + 1], RSTD[:, k:k + 1], ALU.subtract, ALU.mult))
                    dve.wait_ge(bc_loaded, 16 * s.bc_dmas)
                    now(TT(x, x, BC[:, 0:D], ALU.mult))
                    TT(x, x, BC[:, D:2 * D], ALU.add).then_inc(fin_done, 1)
                elif s.kind == "norm0":
                    finish_norm(s)
                elif s.kind == "wo":
                    k = s.fin % 2
                    x = XS[:, k * D:(k + 1) * D]
                    dve.wait_ge(xs_loaded[k], 16 * s.load)
                    dve.wait_ge(bc_loaded, 16 * s.bc_dmas)
                    for h in range(2):
                        dve.wait_ge(pj_full, s.pj[h] + 1)
                        xh, th = x[:, 512 * h:512 * h + 512], TMP[:, 512 * h:512 * h + 512]
                        TT(th, PJ[:, s.pj[h] % 2, :], BC[:, 2 * D + 512 * h:2 * D + 512 * h + 512], ALU.mult).then_inc(pj_free, 1)
                        settle()
                        y = TT(xh, xh, th, ALU.add)
                    y.then_inc(std_in, 1)
                    finish_norm(s)
                elif s.kind == "combine":
                    k = s.fin % 2
                    x = XS[:, k * D:(k + 1) * D]
                    y0, y1 = YG[k][:, 0, :], YG[k][:, 1, :]
                    dve.wait_ge(xs_loaded[k], 16 * s.load)
                    dve.wait_ge(yg_loaded[k], 32 * s.gat[k])
                    dve.wait_ge(bc_loaded, 16 * s.bc_dmas)
                    now(TS(y0, y0, W12[:, s.t:s.t + 1], None, ALU.mult))
                    now(STT(y0, y1, W12[:, 6 + s.t:7 + s.t], y0, ALU.mult, ALU.add))
                    now(TT(y0, y0, BC[:, 2 * D:3 * D], ALU.mult))
                    TT(x, x, y0, ALU.add).then_inc(std_in, 1)
                    finish_norm(s)
                elif s.kind == "layer2":
                    settle()
                    for keys in (KROT, KCTX):
                        halves = keys.rearrange("p (j m) n -> p j m n", m=2)
                        memset(halves[HD:P, :, 0], 0.0)
                        now(memset(halves[0:HD, :, 1], 0.0))
                    dve.wait_ge(layer_loaded, 16 * s.loaded)
                    if s.l % 3 == 0:
                        TS(SINKROW, SINKROW, -1.0, None, ALU.mult).then_inc(sink_ready, 1)
                    else:
                        now(TS(GSUB[:, 0:HD], GSUB[:, 0:HD], -SCALE, None, ALU.mult))
                elif s.kind == "qkv":
                    dve.wait_ge(pj_full, s.pj + 1)
                    bank = PJ[:, s.pj % 2, :]
                    t, c = s.t, s.c
                    heads = 8 if c < 2 else 4
                    n = heads * HD
                    base = stage(s.stg[0])
                    o = 256 if c == 2 and t < XT_TILES else 0
                    plain = STG[:, base + o:base + o + n]
                    if c == 2:
                        tensor_copy(V2[:, t], bank[:, 256:512])
                    if s.l % 3 == 1:
                        raw, sq = TMP[:, 0:n], TMP[:, 512:512 + n]
                        tensor_copy(raw, bank[:, 0:n]).then_inc(pj_free, 1)
                        settle()
                        now(TT(sq, raw, raw, ALU.mult))
                        now(tensor_reduce(QN[:, 0:heads], sq.rearrange("p (h d) -> p h d", d=HD), AX.X, ALU.add))
                        TS(QN[:, 8:8 + heads], QN[:, 0:heads], 1.0 / HD, None, ALU.mult).then_inc(qn_in, 1)
                        dve.wait_ge(qn_std, s.qn)
                        now(reciprocal(QN[:, 24:24 + heads], QN[:, 16:16 + heads]))
                        raw3 = raw.rearrange("p (h d) -> p h d", d=HD)
                        now(TT(raw3, raw3, QN[:, 24:24 + heads].unsqueeze(2).to_broadcast([P, heads, HD]), ALU.mult))
                        gain = GSUB[:, 0:HD] if c < 2 else GSUB[:, HD:2 * HD]
                        if c < 2:
                            for g in range(2):
                                x = TT(plain.rearrange("p (r g d) -> p g r d", r=4, g=2)[:, g],
                                       raw.rearrange("p (g r d) -> p g r d", g=2, r=4)[:, g],
                                       gain.unsqueeze(1).to_broadcast([P, 4, HD]), ALU.mult)
                        else:
                            x = TT(plain.rearrange("p (h d) -> p h d", d=HD), raw3, gain.unsqueeze(1).to_broadcast([P, 4, HD]),
                                   ALU.mult)
                    elif c < 2:
                        x = TS(plain.rearrange("p (r g d) -> p g r d", r=4, g=2),
                               bank.rearrange("p (g r d) -> p g r d", g=2, r=4), -SCALE, None, ALU.mult)
                        x.then_inc(pj_free, 1)
                        settle()
                        x = None
                    else:
                        tensor_copy(plain, bank[:, 0:256]).then_inc(pj_free, 1)
                        settle()
                        x = None
                    if x is not None:
                        now(x)
                    if c < 2 or t >= XT_TILES:
                        v.increment(dve, stg_ready, 1)
                    if t < XT_TILES:
                        b2 = stage(s.stg[1]) if c < 2 else base
                        rotate(plain, STG[:, b2:b2 + n], heads, t, 1.0, 16).then_inc(stg_ready, 1)
                elif s.kind == "route":
                    T = s.tiles
                    R = RT
                    n32, n4 = T * EXPERTS, T * GROUPS
                    bank = PJ[:, s.pj[0] % 2, :]
                    lg = bank[:, 0:T * ROUTER].rearrange("p (t n) -> p t n", n=ROUTER)

                    def by(name, n):
                        return R[name][:, 0:T * n].rearrange("p (t n) -> p t n", n=n)

                    def spread(a, n):
                        return a.unsqueeze(2).to_broadcast([P, T, n])

                    def table(a, n):
                        return a.unsqueeze(1).to_broadcast([P, T, n])

                    def first_best(values, best, n, table_, out_):
                        v3 = by("eq", n)
                        now(TT(v3, values, spread(best, n), ALU.is_equal))
                        now(TT(v3, v3, table(table_, n), ALU.mult))
                        now(tensor_reduce(R["t1"][:, 0:T], v3, AX.X, ALU.max))
                        now(TT(out_, v3, spread(R["t1"][:, 0:T], n), ALU.is_equal))

                    dve.wait_ge(pj_full, s.pj[0] + 1)
                    tensor_copy(by("g4", 4), lg[:, :, 0:GROUPS])
                    tensor_copy(by("l", 32), lg[:, :, GROUPS:ROUTER]).then_inc(pj_free, 1)
                    settle()
                    now(tensor_reduce(R["t0"][:, 0:T], by("g4", 4), AX.X, ALU.max))
                    TT(by("ge", 4), by("g4", 4), spread(R["t0"][:, 0:T], 4), ALU.subtract).then_inc(rt_in, 1)
                    first_best(by("g4", 4), R["t0"][:, 0:T], 4, D4T, by("oh4", 4))
                    now(TS(R["oh4"][:, 0:n4], R["oh4"][:, 0:n4], -1.0, BIG, ALU.add, ALU.mult))
                    l4 = R["l"][:, 0:n32].rearrange("p (t n) -> p t n", n=PER_GROUP)
                    now(TT(l4, l4, R["oh4"][:, 0:n4].unsqueeze(2).to_broadcast([P, n4, PER_GROUP]), ALU.add))
                    now(tensor_reduce(R["m1"][:, 0:T], by("l", 32), AX.X, ALU.max))
                    first_best(by("l", 32), R["m1"][:, 0:T], 32, D32T, by("oh1", 32))
                    now(STT(R["l"][:, 0:n32], R["oh1"][:, 0:n32], -3 * BIG, R["l"][:, 0:n32], ALU.mult, ALU.add))
                    now(tensor_reduce(R["m2"][:, 0:T], by("l", 32), AX.X, ALU.max))
                    first_best(by("l", 32), R["m2"][:, 0:T], 32, D32T, by("oh2", 32))
                    TT(MASKB[:, 0:n32], R["oh1"][:, 0:n32], R["oh2"][:, 0:n32], ALU.add).then_inc(mask_ready, 1)
                    dve.wait_ge(rt_exp, 2 * s.l + 1)
                    now(tensor_reduce(R["t0"][:, 0:T], by("ge", 4), AX.X, ALU.add))
                    now(reciprocal(R["t0"][:, 0:T], R["t0"][:, 0:T]))
                    TT(R["e2"][:, 0:T], R["m2"][:, 0:T], R["m1"][:, 0:T], ALU.subtract).then_inc(rt_in, 1)
                    dve.wait_ge(rt_exp, 2 * s.l + 2)
                    now(TS(R["t1"][:, 0:T], R["e2"][:, 0:T], 1.0, None, ALU.add))
                    now(reciprocal(R["t1"][:, 0:T], R["t1"][:, 0:T]))
                    now(TT(W12[:, 0:T], R["t0"][:, 0:T], R["t1"][:, 0:T], ALU.mult))
                    now(TT(W12[:, 6:6 + T], W12[:, 0:T], R["e2"][:, 0:T], ALU.mult))
                    bank = PJ[:, s.pj[1] % 2, :]
                    dve.wait_ge(pj_full, s.pj[1] + 1)
                    tensor_copy(R["cn"], bank[:, n32:n32 + EXPERTS])
                    tensor_copy(R["rk"][:, 0:n32], bank[:, 0:n32]).then_inc(pj_free, 1)
                    settle()
                    now(TS(R["nb"], R["cn"], float(P), None, ALU.is_gt))
                    for m in range(2, T):
                        now(STT(R["nb"], R["cn"], float(P * m), R["nb"], ALU.is_gt, ALU.add))
                    now(scan(R["incl"], onesF[:, 0:EXPERTS], R["nb"], 0.0, ALU.mult, ALU.add))
                    now(TT(R["ob"], R["incl"], R["nb"], ALU.subtract))
                    now(TS(R["ob"], R["ob"], float(EXPERTS - 1), float(P), ALU.add, ALU.mult))
                    now(TS(R["mb"], U32T, float(P), None, ALU.mult))
                    for k, oh in enumerate(("oh1", "oh2")):
                        for dst, src in (("r", None), ("o", "ob"), ("m", "mb")):
                            now(TT(by("eq", 32), by(oh, 32), by("rk", 32) if src is None else table(R[src], 32), ALU.mult))
                            now(tensor_reduce(R[dst][:, 0:T], by("eq", 32), AX.X, ALU.add))
                        now(TT(R["o"][:, 0:T], R["o"][:, 0:T], R["m"][:, 0:T], ALU.subtract))
                        now(STT(R["o"][:, 0:T], R["r"][:, 0:T], float(P), R["o"][:, 0:T], ALU.is_ge, ALU.mult))
                        now(TT(R["o"][:, 0:T], R["o"][:, 0:T], R["m"][:, 0:T], ALU.add))
                        now(TT(DEST[:, 6 * k:6 * k + T], R["o"][:, 0:T], R["r"][:, 0:T], ALU.add))
                    v.increment(dve, dest_ready, 1)
                    ov = R["eq32"].rearrange("p (j e) -> p j e", e=EXPERTS)
                    now(TT(ov, R["incl"].unsqueeze(1).to_broadcast([P, MAX_OVER, EXPERTS]),
                           OVT.unsqueeze(2).to_broadcast([P, MAX_OVER, EXPERTS]), ALU.is_le))
                    now(tensor_reduce(R["be"], ov, AX.X, ALU.add))
                    now(TS(OVI[:, 0:MAX_OVER], R["be"], float(EXPERTS - 1), None, ALU.min))
                    now(tensor_copy(OVI[:, MAX_OVER:MAX_OVER + 1], R["incl"][:, EXPERTS - 1:EXPERTS]))
                    dve.wait_ge(pj_full, s.pj[2] + 1)
                    tensor_copy(IDX, PJ[:, s.pj[2] % 2, 0:BLOCKS]).then_inc(pj_free, 1)
                    settle()
                    v.increment(dve, idx_ready, 1)
                elif s.kind == "moe":
                    T0, S0, J0 = s.tr[0], s.sc[0], s.pj[0]

                    def hidden(at_, r, first=False):
                        dve.wait_ge(sc_free, at_(2, S0 + r + 1))
                        if not first:
                            dve.wait_ge(tr_full, at_(6, T0 + 3 * r - 1))
                        TT(HID[r % 2], GSI[r % 2], UPS[r % 2], ALU.mult).then_inc(hid_ready, 1)

                    def rows(at_, r, first=False):
                        for h in range(2):
                            use = J0 + 2 * r + h
                            dve.wait_ge(pj_full, at_(4, use + 1))
                            if not first and h == 0:
                                dve.wait_ge(y_stored[r % 2], at_(16, s.y0 + 16 * (r // 2)))
                            tensor_copy(YR[r % 2][:, h * 512:(h + 1) * 512], PJ[:, use % 2, :]).then_inc(pj_free, 1)

                    once = lambda a, b: b
                    hidden(once, 0, first=True)
                    hidden(once, 1, first=True)
                    rows(once, 0, first=True)
                    hidden(once, 2)
                    rows(once, 1, first=True)
                    hidden(once, 3)
                    rows(once, 2)
                    rounds = EXPERTS // 2 - 2
                    with dve.Fori(0, rounds) as i:
                        for r in (3, 4):
                            hidden(lambda a, b: i * a + b, r + 1)
                            rows(lambda a, b: i * a + b, r)
                    rows(once, EXPERTS - 1)
                    v.count[pj_free.name] += 4 * (rounds - 1)
                    v.count[hid_ready.name] += 2 * (rounds - 1)
                    v.latest = (pj_free, v.count[pj_free.name])
                    o = over[s.l]
                    count = dve.value_load(OVI[0:1, MAX_OVER:MAX_OVER + 1], min_val=0, max_val=MAX_OVER)
                    with dve.Fori(0, MAX_OVER) as j:
                        with dve.If(j < count):
                            dve.wait_ge(o["act"], j + 1)
                            TT(HID[0], GSI[0], UPS[0], ALU.mult).then_inc(o["hid"], 1)
                            dve.wait_ge(o["down"], j + 2)
                            dve.wait_ge(o["free"], j + 1)
                            tensor_copy(YR[0][:, 0:512], PJ[:, 0, :])
                            tensor_copy(YR[0][:, 512:1024], PJ[:, 1, :]).then_inc(o["y"], 1)
                    v.latest = (pj_free, v.count[pj_free.name])

        @block.gpsimd
        def _(pool):
            dma = pool.dma_start
            C = ins["constants"]

            def const(name):
                return C[:, CONST[name][0]:CONST[name][1]]

            def rows(a, n=P):
                return a.unsqueeze(0).to_broadcast([n, a.shape[-1]])

            x_in, ctx_in, out_rows = (a.rearrange("b s d -> (b s) d") for a in (ins["x"], ins["ctx_2"], out))
            dma(KF[:, :], C[:, 0:4 * P]).then_inc(consts_loaded, 16)
            dma(G[:, 0:2 * P], C[:, CONST["below"][0]:CONST["before"][1]]).then_inc(consts_loaded, 16)
            dma(ROPE[:, :], const("rope1")).then_inc(consts_loaded, 16)
            dma(TABLES, C[:, CONST["tok"][0]:CONST["over"][1]]).then_inc(consts_loaded, 16)
            with nc.allow_non_contiguous_dma(reason="conditioning vectors onto partitions, 8 KB"):
                scr = SCR.rearrange("p (c r) -> p c r", r=2)
                for r, a in enumerate((ins["c_2"][0], ins["c_ctx_2"])):
                    dma(scr[:, :, r], a.rearrange("(c p) -> p c", p=P)).then_inc(c_loaded, 16)

            for o in over:
                pool.sem_inc(o["turned"], 1)
                pool.sem_inc(o["down"], 1)
                pool.sem_inc(o["free"], 1)

            loaded_fins = set()

            def x_slot_free(f):
                prev = by_fin.get(f.fin - 2)
                if prev is None:
                    return
                if prev.q:
                    pool.wait_ge(fin_done, prev.q)
                if prev.turned is not None:
                    pool.wait_ge(tr_full, prev.turned + 1)
                if prev.xst[f.fin % 2]:
                    pool.wait_ge(x_stored[f.fin % 2], 16 * prev.xst[f.fin % 2])

            def load_fin(f):
                if f.fin in loaded_fins:
                    return
                loaded_fins.add(f.fin)
                x_slot_free(f)
                k = f.fin % 2
                r = slice(f.t * P, (f.t + 1) * P)
                if f.kind == "open" or (f.kind == "wout" and f.l == 0):
                    src = x_in[r, :]
                elif f.kind in ("norm0", "wo") and f.l == 0 and f.t >= XT_TILES:
                    src = ctx_in[(f.t - XT_TILES) * P:(f.t - XT_TILES + 1) * P, :]
                else:
                    src = XD[r, :]
                dma(XS[:, k * D:(k + 1) * D], src).then_inc(xs_loaded[k], 16)
                if f.kind == "combine":
                    prev = by_fin[f.fin - 2]
                    if prev.kind == "combine":
                        pool.wait_ge(fin_done, prev.q)
                    for j in range(2):
                        pool.indirect_dma_start(YG[k][:, j, :], None, YD[:, :],
                                                bass.IndirectOffsetOnAxis(ap=DEST[:, 6 * j + f.t:6 * j + f.t + 1], axis=0)
                                                ).then_inc(yg_loaded[k], 16)

            def group_start(f):
                before = by_fin.get(f.fin - 1)
                if before is not None:
                    for k in range(2):
                        if before.xst[k]:
                            pool.wait_ge(x_stored[k], 16 * before.xst[k])

            def store_fin(f):
                k = f.fin % 2
                r = slice(f.t * P, (f.t + 1) * P)
                if f.stores_x or f.stores_h:
                    pool.wait_ge(fin_done, f.q)
                if f.stores_x:
                    dma(XD[r, :], XS[:, k * D:(k + 1) * D]).then_inc(x_stored[k], 16)
                if f.stores_h:
                    dma(HDR[r, :] if f.kind == "wo" else out_rows[r, :], HS[:, k]).then_inc(h_stored[k], 16)

            def fin_step(f):
                prev, nxt = by_fin.get(f.fin - 1), by_fin.get(f.fin + 1)
                if prev is None or prev.kind != f.kind or prev.l != f.l:
                    group_start(f)
                    load_fin(f)
                if nxt is not None and nxt.kind == f.kind and nxt.l == f.l:
                    load_fin(nxt)
                store_fin(f)

            adas = [s for s in steps if s.kind == "ada"]

            def quarter(q, o):
                return XS[32 * q:32 * q + 2, o:o + P]

            def load_ada(s):
                k = s.ada % 2
                o = k * D
                j, l = s.j, s.l
                if s.ada >= 2:
                    pool.wait_ge(mod_stored[k], 64 * (s.ada // 2))
                for q in range(4):
                    c = slice(j * 512 + q * P, j * 512 + (q + 1) * P)
                    dma(quarter(q, o), rows(ins["b_ada_2"][l, c], 2)).then_inc(ada_loaded[k], 16)
                if j // 2 in (1, 4):
                    g = ins["g_attn_2" if j // 2 == 1 else "g_ffn_2"][l, (j % 2) * 512:(j % 2 + 1) * 512]
                    for q in range(4):
                        dma(quarter(q, o + P), rows(g[q * P:(q + 1) * P], 2)).then_inc(ada_loaded[k], 16)

            def load_layer1(l):
                for k, name in enumerate(("lam_q1", "lam_k1", "lam_q2", "lam_k2")):
                    dma(LAMV[:, 64 * k:64 * k + 64], rows(ins[name][l])).then_inc(layer_loaded, 16)
                dma(BFT, rows(ins["b_f"][l])).then_inc(layer_loaded, 16)
                dma(GSUB[:, :], rows(ins["g_subln"][l])).then_inc(layer_loaded, 16)

            last_fin = None
            zeroed = False
            for s in steps:
                if s.kind in FINISHING:
                    fin_step(s)
                    last_fin = s
                    if s.kind == "wout" and s.t == 0 and s.l == 0:
                        load_layer1(1)
                elif s.kind == "layer1":
                    if s.l == 0:
                        load_layer1(0)
                        pool.wait_ge(zeros_ready, 1)
                        dma(IDT.rearrange("(b s) n -> b (s n)", s=P), G[0:BLOCKS, 2 * P:3 * P]).then_inc(idt_zeroed, 16)
                        for b in range(EXPERTS, BLOCKS):
                            dma(YD[b * P:(b + 1) * P, :], BC[:, 0:D]).then_inc(yd_zeroed, 16)
                elif s.kind == "ada":
                    if s.j == 0:
                        for f in (last_fin, by_fin.get(last_fin.fin - 1)):
                            if f.q:
                                pool.wait_ge(fin_done, f.q)
                            if f.turned is not None:
                                pool.wait_ge(tr_full, f.turned + 1)
                        for k in range(2):
                            if last_fin.xst[k]:
                                pool.wait_ge(x_stored[k], 16 * last_fin.xst[k])
                        load_ada(adas[s.ada])
                        load_ada(adas[s.ada + 1])
                    k = s.ada % 2
                    pool.wait_ge(ada_ready, s.ada + 1)
                    for q in range(4):
                        c = slice(s.j * 512 + q * P, s.j * 512 + (q + 1) * P)
                        dma(MOD[s.l, :, c], quarter(q, k * D)).then_inc(mod_stored[k], 16)
                    if s.j < 10:
                        load_ada(adas[s.ada + 2])
                    if s.j == 11:
                        for k in range(2):
                            pool.wait_ge(mod_stored[k], 64 * (s.ada + 1) // 2)
                elif s.kind == "load_bc":
                    if last_fin.q:
                        pool.wait_ge(fin_done, last_fin.q)
                    l, r = s.l, int(s.ctx)

                    def part(ll, j):
                        return rows(MOD[ll, r, j * D:(j + 1) * D])

                    if s.what == "ln":
                        pool.wait_ge(topk_done, 3 * (l + 1))
                        src = [rows(ins["ln_g"][l]), rows(ins["ln_b"][l])]
                    elif s.what == "attn":
                        src = [part(l, 1), part(l, 0)]
                    elif s.what == "ffn":
                        src = [part(l, 4), part(l, 3), part(l, 2)]
                    elif s.what == "next":
                        src = [part(l + 1, 1), part(l + 1, 0), part(l, 5)]
                    else:
                        src = [rows(ins["g_final_2"]), None, part(l, 5)]
                    for k, a in enumerate(src):
                        if a is not None:
                            dma(BC[:, k * D:(k + 1) * D], a).then_inc(bc_loaded, 16)
                elif s.kind == "layer2":
                    l = s.l
                    if last_fin.q:
                        pool.wait_ge(fin_done, last_fin.q)
                    if l % 3 == 0:
                        dma(SINKROW, rows(ins["sink_a_2"][l // 3], 1)).then_inc(layer_loaded, 16)
                        dma(ROPE[:, :], const("rope2")).then_inc(layer_loaded, 16)
                    else:
                        dma(GSUB[:, 0:HD], rows(ins["gq_b_2"][l // 3])).then_inc(layer_loaded, 16)
                        dma(GSUB[:, HD:2 * HD], rows(ins["gk_b_2"][l // 3])).then_inc(layer_loaded, 16)
                    rw = RWT.rearrange("p (c n) -> p c n", n=ROUTER)
                    dma(rw[:, :, 0:GROUPS], ins["w_group_2"][l].rearrange("(c p) n -> p c n", p=P)).then_inc(router_loaded, 16)
                    dma(rw[:, :, GROUPS:ROUTER], ins["w_router_2"][l].rearrange("(c p) n -> p c n", p=P)).then_inc(
                        router_loaded, 16)
                    dma(RB[0:1, 0:GROUPS], rows(ins["b_group_2"][l], 1)).then_inc(router_loaded, 16)
                    dma(RB[0:1, GROUPS:ROUTER], rows(ins["b_router_2"][l], 1)).then_inc(router_loaded, 16)
                elif s.kind == "route":
                    for k in range(2):
                        pool.wait_ge(h_stored[k], 16 * last_fin.hst[k])
                    if s.l == 0:
                        pool.wait_ge(idt_zeroed, 16)
                    pool.wait_ge(dest_ready, s.l + 1)
                    for k in range(2):
                        for t in range(s.tiles):
                            pool.indirect_dma_start(
                                IDT[:, :], bass.IndirectOffsetOnAxis(ap=DEST[:, 6 * k + t:6 * k + t + 1], axis=0),
                                TOK[:, t:t + 1], None).then_inc(ids_stored, 16)
                    total_ids[0] += 2 * s.tiles
                    pool.wait_ge(ids_stored, 16 * total_ids[0])
                    dma(STG[0:BLOCKS, 0:P], IDT.rearrange("(b s) n -> b (s n)", s=P)).then_inc(ids_loaded, 16)
                elif s.kind == "moe":
                    T0, J0 = s.tr[0], s.pj[0]
                    gathers0 = 34 * s.l

                    def gather(at_, r, e):
                        par = r % 2
                        if r >= 2:
                            pool.wait_ge(tr_full, at_(6, T0 + (3 * (r - 2) if r > 2 else 1) + 1))
                        nc.gpsimd.tensor_copy(XI[:, par:par + 1], IDX[:, e]).then_inc(pool_done, 1)
                        pool.wait_ge(pool_done, at_(2, gathers0 + r + 1))
                        pool.sem_inc(gather_started, 1)
                        pool.indirect_dma_start(XE[par], None, HDR[:, :],
                                                bass.IndirectOffsetOnAxis(ap=XI[:, par:par + 1], axis=0)
                                                ).then_inc(xe_loaded[par], 16)

                    def store(at_, r, dst):
                        pool.wait_ge(pj_free, at_(4, J0 + 2 * r + 2))
                        dma(dst, YR[r % 2]).then_inc(y_stored[r % 2], 16)

                    once = lambda a, b: b
                    pool.wait_ge(idx_ready, s.l + 1)
                    for e in range(4):
                        gather(once, e, slice(e, e + 1))
                    store(once, 0, YD[0:P, :])
                    with pool.Fori(0, EXPERTS // 2 - 1) as i:
                        for r in (1, 2):
                            gather(lambda a, b: i * a + b, r + 3, bass.ds(i * 2 + (r + 3), 1))
                            store(lambda a, b: i * a + b, r, YD[bass.ds(i * (2 * P) + r * P, P), :])
                    store(once, EXPERTS - 1, YD[(EXPERTS - 1) * P:EXPERTS * P, :])
                    for k in range(2):
                        pool.wait_ge(xe_loaded[k], s.xe0[k] + 16 * 17)
                        pool.wait_ge(y_stored[k], s.y0 + 256)
                    o = over[s.l]
                    pool.wait_ge(pj_full, s.pj[-1] + 1)
                    count = pool.value_load(OVI[0:1, MAX_OVER:MAX_OVER + 1], min_val=0, max_val=MAX_OVER)
                    with pool.Fori(0, MAX_OVER) as j:
                        with pool.If(j < count):
                            pool.wait_ge(o["turned"], j + 1)
                            nc.gpsimd.tensor_copy(XI[:, 0:1], IDX[:, bass.ds(j + EXPERTS, 1)]).then_inc(o["ix"], 1)
                            pool.wait_ge(o["ix"], j + 1)
                            pool.sem_inc(gather_started, 1)
                            pool.indirect_dma_start(XE[0], None, HDR[:, :],
                                                    bass.IndirectOffsetOnAxis(ap=XI[:, 0:1], axis=0)).then_inc(o["x"], 16)
                            pool.wait_ge(o["y"], j + 1)
                            dma(YD[bass.ds(j * P + EXPERTS * P, P), :], YR[0]).then_inc(o["stored"], 16)
                            pool.wait_ge(o["stored"], j * 16 + 16)
                            pool.sem_inc(o["free"], 1)
            for k in range(2):
                if last_fin.xst[k]:
                    pool.wait_ge(x_stored[k], 16 * last_fin.xst[k])
                if last_fin.hst[k]:
                    pool.wait_ge(h_stored[k], 16 * last_fin.hst[k])


_INS = ['x', 'w_in', 'b_f', 'lam_q1', 'lam_k1', 'lam_q2', 'lam_k2', 'g_subln', 'w_out', 'ln_g', 'ln_b', 'c_2', 'ctx_2',
        'c_ctx_2', 'w_ada_2', 'b_ada_2', 'g_attn_2', 'w_qkv_2', 'w_o_2', 'sink_a_2', 'gq_b_2', 'gk_b_2',
        'g_ffn_2', 'w_group_2', 'b_group_2', 'w_router_2', 'b_router_2', 'w_gate_2', 'w_up_2', 'w_down_2', 'g_final_2']


def kernel(**inputs):
    import numpy as _np
    import concourse.bacc as _bacc
    from concourse import mybir as _mybir
    from concourse.bass_utils import run_bass_kernel_spmd as _run

    nc = _bacc.Bacc("TRN2", target_bir_lowering=False, num_devices=1)
    arrays, args = {}, {}
    for name in _INS + ["constants"]:
        a = CONSTANTS if name == "constants" else _np.ascontiguousarray(inputs[name])
        arrays[f"in_{name}_dram"] = a
        args[name] = nc.dram_tensor(f"in_{name}_dram", a.shape, _mybir.dt.from_np(a.dtype), kind="ExternalInput").ap()
    out = nc.dram_tensor("out_0_dram", (1, SEQ, D), F32, kind="ExternalOutput").ap()
    build(nc, args, out)
    r = _run(nc, [arrays], core_ids=[0])
    return r.results[0]["out_0_dram"]
```
